# Optimizing a Trainium2 kernel written in Bass

```python
import math
import jax, jax.numpy as jnp
from jax import lax
import numpy as np

D_MODEL = 1024
BATCH = 1
SEQ = 1024
DEPTH = 1

HEAD_DIM = 64
D_MIX = D_MODEL
SSM_GROUP = 16
SSM_WIDTH = D_MIX // 4
SSM_GROUPS = SSM_WIDTH // SSM_GROUP
SSM_STATE = 64
DSA_HEADS = (D_MIX - SSM_WIDTH) // (2 * HEAD_DIM)
FOX_HEADS = DSA_HEADS
DSA_WIDTH = DSA_HEADS * HEAD_DIM
FOX_WIDTH = FOX_HEADS * HEAD_DIM
DSA_PATTERNS = ((128, 1), (512, 4), (2048, 16))
DSA_BLOCK = 128
FOX_BLOCK = 128
D_FF = ((8 * D_MODEL // 3 + 255) // 256) * 256
IN_SIZES = (SSM_WIDTH, 3 * DSA_WIDTH, 3 * FOX_WIDTH, FOX_HEADS)
N_IN = sum(IN_SIZES)
RMS_EPS = 1e-6

kernel_name = 'hybrid_s5_dilated_fox_block'

def rms_norm(x, g):
    xf = x.astype(jnp.float32)
    y = xf * lax.rsqrt(jnp.mean(xf * xf, axis=-1, keepdims=True) + RMS_EPS)
    return (y * g.astype(jnp.float32)).astype(x.dtype)

def _complex_affine_combine(e1, e2):
    a1r, a1i, b1r, b1i = e1
    a2r, a2i, b2r, b2i = e2
    ar = a2r * a1r - a2i * a1i
    ai = a2r * a1i + a2i * a1r
    br = a2r * b1r - a2i * b1i + b2r
    bi = a2r * b1i + a2i * b1r + b2i
    return (ar, ai, br, bi)

def s5_mixer(u, log_dt, a_re, a_im, b_re, b_im, c_re, c_im, d_skip, w_glu, b_glu):
    bsz, seq, _ = u.shape
    dtype = u.dtype
    f32 = jnp.float32
    dt = jnp.exp(log_dt.astype(f32))[:, None]
    ar, ai = a_re.astype(f32), a_im.astype(f32)
    decay = jnp.exp(ar * dt)
    abar_re = decay * jnp.cos(ai * dt)
    abar_im = decay * jnp.sin(ai * dt)
    mag2 = ar * ar + ai * ai
    coef_re = ((abar_re - 1.0) * ar + abar_im * ai) / mag2
    coef_im = (abar_im * ar - (abar_re - 1.0) * ai) / mag2
    br, bi = b_re.astype(f32), b_im.astype(f32)
    bbar_re = coef_re[..., None] * br - coef_im[..., None] * bi
    bbar_im = coef_re[..., None] * bi + coef_im[..., None] * br
    ug = u.reshape(bsz, seq, SSM_GROUPS, SSM_GROUP)
    x_re = jnp.einsum('bsgc,gpc->sbgp', ug, bbar_re.astype(dtype))
    x_im = jnp.einsum('bsgc,gpc->sbgp', ug, bbar_im.astype(dtype))
    shape = x_re.shape
    elems = (jnp.broadcast_to(abar_re.astype(dtype), shape),
             jnp.broadcast_to(abar_im.astype(dtype), shape), x_re, x_im)
    _, _, h_re, h_im = lax.associative_scan(_complex_affine_combine, elems, axis=0)
    y = (jnp.einsum('sbgp,gcp->bsgc', h_re, c_re)
         - jnp.einsum('sbgp,gcp->bsgc', h_im, c_im))
    y = y.reshape(bsz, seq, SSM_WIDTH) + d_skip * u
    g = jax.nn.gelu(y)
    return g * jax.nn.sigmoid(g @ w_glu + b_glu)

def dilated_window_branch(q, k, v, window, dilation):
    bsz, seq, nh, dh = q.shape
    span = window // dilation
    blk = DSA_BLOCK
    length = seq // dilation
    nb = -(-length // blk)
    lp = nb * blk

    def to_strided(t):
        t = t.reshape(bsz, length, dilation, nh, dh)
        return jnp.pad(t, ((0, 0), (0, lp - length), (0, 0), (0, 0), (0, 0)))

    def key_blocks(t):
        t = jnp.pad(to_strided(t), ((0, 0), (blk, 0), (0, 0), (0, 0), (0, 0)))
        t = t.reshape(bsz, nb + 1, blk, dilation, nh, dh)
        return jnp.concatenate([t[:, :-1], t[:, 1:]], axis=2)

    qs = to_strided(q).reshape(bsz, nb, blk, dilation, nh, dh)
    ks, vs = key_blocks(k), key_blocks(v)
    s = jnp.einsum('bnqrhd,bnkrhd->bnrhqk', qs, ks).astype(jnp.float32)
    qi = jnp.arange(blk)[:, None]
    ki = jnp.arange(2 * blk)[None, :]
    dist = blk + qi - ki
    key_row = (jnp.arange(nb) * blk - blk)[:, None, None] + ki[None]
    valid = (dist >= 0) & (dist <= span) & (key_row >= 0)
    s = jnp.where(valid[None, :, None, None], s, -jnp.inf)
    m = jnp.max(s, axis=-1, keepdims=True)
    p = jnp.exp(s - m)
    den = jnp.sum(p, axis=-1, keepdims=True)
    o = jnp.einsum('bnrhqk,bnkrhd->bnqrhd', (p / den).astype(v.dtype), vs)
    lse = (m + jnp.log(den))[..., 0]
    o = o.reshape(bsz, lp, dilation, nh, dh)[:, :length].reshape(bsz, seq, nh, dh)
    lse = lse.transpose(0, 1, 4, 2, 3).reshape(bsz, lp, dilation, nh)[:, :length]
    return o, lse.reshape(bsz, seq, nh)

def dilated_attention(q, k, v):
    results = [dilated_window_branch(q, k, v, w, d) for (w, d) in DSA_PATTERNS]
    outs = jnp.stack([r[0] for r in results], axis=0)
    lses = jnp.stack([r[1] for r in results], axis=0)
    wts = jax.nn.softmax(lses, axis=0).astype(q.dtype)
    return jnp.einsum('pbsh,pbshd->bshd', wts, outs)

def forgetting_attention(q, k, v, log_f):
    bsz, seq, nh, dh = q.shape
    cum = jnp.cumsum(log_f, axis=1).transpose(0, 2, 1)
    outs = []
    for i in range(seq // FOX_BLOCK):
        q0, q1 = i * FOX_BLOCK, (i + 1) * FOX_BLOCK
        s = jnp.einsum('bqhd,bkhd->bhqk', q[:, q0:q1], k[:, :q1]).astype(jnp.float32)
        bias = cum[:, :, q0:q1, None] - cum[:, :, None, :q1]
        causal = jnp.arange(q0, q1)[:, None] >= jnp.arange(q1)[None, :]
        p = jax.nn.softmax(jnp.where(causal, s + bias, -jnp.inf), axis=-1)
        outs.append(jnp.einsum('bhqk,bkhd->bqhd', p.astype(v.dtype), v[:, :q1]))
    return jnp.concatenate(outs, axis=1)

def setup_inputs(seed: int = 0) -> dict:
    key = jax.random.key(seed)
    ks = jax.random.split(key, 24)
    f32 = jnp.float32
    L, D, G, P, C = DEPTH, D_MODEL, SSM_GROUPS, SSM_STATE, SSM_GROUP

    def nrm(k, shape, scale):
        return jax.random.normal(k, shape, f32) * scale

    def gain(k, shape):
        return 1.0 + 0.02 * jax.random.normal(k, shape, f32)

    n_idx = jnp.arange(P, dtype=f32)
    return {
        'x': jax.random.normal(ks[0], (BATCH, SEQ, D), f32),
        'g_pre_mix': gain(ks[1], (L, D)),
        'w_in': nrm(ks[2], (L, D, N_IN), D ** -0.5),
        'b_f': 1.0 + 3.0 * jax.random.uniform(ks[3], (L, FOX_HEADS), f32),
        'ssm_log_dt': jax.random.uniform(ks[4], (L, G), f32, math.log(1e-3), math.log(1e-1)),
        'ssm_a_re': -0.5 + 0.01 * jax.random.normal(ks[5], (L, G, P), f32),
        'ssm_a_im': math.pi * n_idx + 0.01 * jax.random.normal(ks[6], (L, G, P), f32),
        'ssm_b_re': nrm(ks[7], (L, G, P, C), (2 * C) ** -0.5),
        'ssm_b_im': nrm(ks[8], (L, G, P, C), (2 * C) ** -0.5),
        'ssm_c_re': nrm(ks[9], (L, G, C, P), (2 * P) ** -0.5),
        'ssm_c_im': nrm(ks[10], (L, G, C, P), (2 * P) ** -0.5),
        'ssm_d': nrm(ks[11], (L, SSM_WIDTH), 1.0),
        'w_glu': nrm(ks[12], (L, SSM_WIDTH, SSM_WIDTH), SSM_WIDTH ** -0.5),
        'b_glu': nrm(ks[13], (L, SSM_WIDTH), 0.01),
        'g_mix': gain(ks[14], (L, D_MIX)),
        'w_out': nrm(ks[15], (L, D_MIX, D), D_MIX ** -0.5),
        'g_post_mix': gain(ks[16], (L, D)),
        'g_pre_ffn': gain(ks[17], (L, D)),
        'w_gate_up': nrm(ks[18], (L, D, 2 * D_FF), D ** -0.5),
        'w_down': nrm(ks[19], (L, D_FF, D), D_FF ** -0.5),
        'g_post_ffn': gain(ks[20], (L, D)),
    }

def reference(x, g_pre_mix, w_in, b_f, ssm_log_dt, ssm_a_re, ssm_a_im, ssm_b_re, ssm_b_im,
              ssm_c_re, ssm_c_im, ssm_d, w_glu, b_glu, g_mix, w_out, g_post_mix,
              g_pre_ffn, w_gate_up, w_down, g_post_ffn):
    bsz, seq, _ = x.shape
    scale = HEAD_DIM ** -0.5
    offsets = [int(o) for o in np.cumsum(IN_SIZES)[:-1]]
    for l in range(DEPTH):
        h = rms_norm(x, g_pre_mix[l])
        proj = h @ w_in[l]
        u_ssm, qkv_dsa, qkv_fox, f_logit = jnp.split(proj, offsets, axis=-1)

        y_ssm = s5_mixer(u_ssm, ssm_log_dt[l], ssm_a_re[l], ssm_a_im[l], ssm_b_re[l],
                         ssm_b_im[l], ssm_c_re[l], ssm_c_im[l], ssm_d[l], w_glu[l], b_glu[l])

        qkv_dsa = qkv_dsa.reshape(bsz, seq, 3, DSA_HEADS, HEAD_DIM)
        y_dsa = dilated_attention(qkv_dsa[:, :, 0] * scale, qkv_dsa[:, :, 1], qkv_dsa[:, :, 2])

        qkv_fox = qkv_fox.reshape(bsz, seq, 3, FOX_HEADS, HEAD_DIM)
        log_f = jax.nn.log_sigmoid((f_logit + b_f[l]).astype(jnp.float32))
        y_fox = forgetting_attention(qkv_fox[:, :, 0] * scale, qkv_fox[:, :, 1],
                                     qkv_fox[:, :, 2], log_f)

        gm = g_mix[l]
        mixed = jnp.concatenate([
            rms_norm(y_ssm, gm[:SSM_WIDTH]),
            rms_norm(y_dsa.reshape(bsz, seq, DSA_WIDTH), gm[SSM_WIDTH:SSM_WIDTH + DSA_WIDTH]),
            rms_norm(y_fox.reshape(bsz, seq, FOX_WIDTH), gm[SSM_WIDTH + DSA_WIDTH:]),
        ], axis=-1)
        x = x + rms_norm(mixed @ w_out[l], g_post_mix[l])

        h = rms_norm(x, g_pre_ffn[l])
        gate, up = jnp.split(h @ w_gate_up[l], 2, axis=-1)
        x = x + rms_norm((jax.nn.silu(gate) * up) @ w_down[l], g_post_ffn[l])
    return x


_drawn_inputs = setup_inputs


def setup_inputs(seed=0):
    import zlib

    import numpy as np

    out = dict(_drawn_inputs(seed))
    spreads = {}
    factors = {'ssm_a_re': 8.0,
     'ssm_b_re': 3.358,
     'ssm_b_im': 3.402,
     'ssm_c_re': 3.332,
     'ssm_c_im': 3.374,
     'b_glu': 8.0,
     'g_mix': 3.541,
     'g_post_mix': 3.493,
     'g_pre_ffn': 3.466,
     'g_post_ffn': 5.126}
    for name, (base, spread) in spreads.items():
        noise = np.random.default_rng([zlib.crc32(name.encode()), seed]).standard_normal(out[name].shape)
        drawn = base * np.exp(spread * noise) if base else spread * noise
        out[name] = __import__('jax').numpy.asarray(drawn.astype(out[name].dtype))
    for name, factor in factors.items():
        out[name] = (out[name] * factor).astype(out[name].dtype)
    return out
```

```python
import math
from contextlib import ExitStack

import numpy as np

import concourse.bass as bass
from concourse import mybir

P = 128
D = 1024
SEQ = 1024
KT = D // P
NT = SEQ // P
HALF = 512
DH = 64
NH = 6
SSM_W = 256
G, CH, ST = 16, 16, 64
TS = 8
NC = SEQ // TS
NJ = G // 2
ATT_W = NH * DH
D_FF = 2816
FT = D_FF // P
PARTS = (8, 8, 6)
UF = SSM_W + NH
VW = 256
NV = 2 * ATT_W // VW
EPS = 1e-6
MASKED = -1e30
QB = 2
UNITS = NT // QB
ORDER = (3, 0, 2, 1)
PLACE = tuple(ORDER.index(g) for g in range(UNITS))
LNC_W = SEQ - P + QB * P
PCS = UNITS * (UNITS + 1) // 2
PR_W = QB * QB * P * PCS

C_QK = 0
C_OUT = C_QK + 4 * NH // 2
C_FFN = C_OUT + KT


class NormSemaphores:

    def __init__(self, sem, name):
        self.sums = sem(name + "_sums")
        self.mean = sem(name + "_mean")
        self.ln = sem(name + "_ln")
        self.seed = sem(name + "_seed")
        self.rstd = sem(name + "_rstd")


class SquareSemaphores:

    def __init__(self, sem, name):
        self.sq = sem(name + "_sq")
        self.added = sem(name + "_added")


def block_kernel(nc, x_t, gains, w_uf, w_v, w_stream, w_last, s_par, s_bc, rows, w_glu, b_f,
                 lnc_dram, out_t):
    f32, f32r, bf16 = mybir.dt.float32, mybir.dt.float32r, mybir.dt.bfloat16
    ALU, ACT, AX = mybir.AluOpType, mybir.ActivationFunctionType, mybir.AxisListType

    ctx = ExitStack()
    with ctx:
        qk_dram = nc.dram_tensor("qk_scratch", (4, NH // 2, P, SEQ), f32, kind="Internal").ap()
        v_dram = nc.dram_tensor("v_scratch", (2 * NH, P, NT, DH), f32, kind="Internal").ap()
        cum_dram = nc.dram_tensor("cum_scratch", (NH, SEQ), f32, kind="Internal").ap()
        x2_dram = nc.dram_tensor("x2_scratch", (P, KT, SEQ), f32, kind="Internal").ap()
        qk_heads = qk_dram.rearrange("a c (b d) n -> a (c b) d n", b=2)

        def sem(name):
            return ctx.enter_context(nc.semaphore(name))

        def sem_list(name, n):
            return [sem(f"{name}{i}") for i in range(n)]

        par_in, gains_in, bf_in, wg_in, row_in, lnc_in = (sem(n) for n in (
            "par_in", "gains_in", "bf_in", "wg_in", "row_in", "lnc_in"))
        x_in, x_again, uf_in = sem_list("x_in", KT), sem_list("x_again", KT), sem_list("uf_in", 2)
        ones_set, ident_set, ident2_set = sem("ones_set"), sem("ident_set"), sem("ident2_set")
        dve_chain, pool_chain, dve_waited = sem("dve_chain"), sem("pool_chain"), sem("dve_waited")
        w_loaded = sem_list("w_loaded", 2)
        w_high, w_split, mm_done, evacuated = (sem(n) for n in ("w_high", "w_split", "mm_done", "evacuated"))
        x_high, x_split, sq_x, sq_added, uf_high, uf_split, uf_mm, uf_copied, uf_scaled = (sem(n) for n in (
            "x_high", "x_split", "sq_x", "sq_added", "uf_high", "uf_split", "uf_mm", "uf_copied", "uf_scaled"))
        v_in, v_high_done, v_split, v_mm, v_scaled, v_out = (sem(n) for n in (
            "v_in", "v_high_done", "v_split", "v_mm", "v_scaled", "v_out"))
        f_mm, f_abs, f_exp, f_ln, f_cum, cum_out = (sem(n) for n in (
            "f_mm", "f_abs", "f_exp", "f_ln", "f_cum", "cum_out"))
        qk_out = sem_list("qk_out", 2)
        par_act, par_dve, powers, ut_mm, ut_out, mt_done, mb_mm, mb_out = (sem(n) for n in (
            "par_act", "par_dve", "powers", "ut_mm", "ut_out", "mt_done", "mb_mm", "mb_out"))
        d_done, e_done, kl_mm, kl_out, tz_in, x_mm, h_done, du_done, y_mm, y_sum = (sem(n) for n in (
            "d_done", "e_done", "kl_mm", "kl_out", "tz_in", "x_mm", "h_done", "du_done", "y_mm", "y_sum"))
        gelu_done, gt_mm, gt_out, glu_mm, glu_sum, glu_sig, y_gated, y_ssm_sq = (sem(n) for n in (
            "gelu_done", "gt_mm", "gt_out", "glu_mm", "glu_sum", "glu_sig", "y_gated", "y_ssm_sq"))
        staged, fb_in = sem_list("staged", 2), sem("fb_in")
        qk_high_done, values_high_done, low_parts_done, qk_done, row_max_done, exp_done, pt_mm, pt_high_done, pt_low_done = (
            sem(n) for n in ("qk_high_done", "values_high_done", "low_parts_done", "qk_done", "row_max_done", "exp_done", "pt_mm",
                             "pt_high_done", "pt_low_done"))
        pv_done, ot_done, yt_mm, rden_done, y_done = (sem(n) for n in (
            "pv_done", "ot_done", "yt_mm", "rden_done", "y_done"))
        y_att_sq, y_scaled, fox_scaled, mix_mm, mix_high, mix_split = (sem(n) for n in (
            "y_att_sq", "y_scaled", "fox_scaled", "mix_mm", "mix_high", "mix_split"))
        zn, x2_done, h2_high, h2_split, x2_out, x2_again = (sem(n) for n in (
            "zn", "x2_done", "h2_high", "h2_split", "x2_out", "x2_again"))
        silu_done, hf_done, hid_high, hid_low = (sem(n) for n in ("silu_done", "hf_done", "hid_high", "hid_low"))
        ze, out_done, out_stored = sem("ze"), sem("out_done"), sem("out_stored")
        n1s_norm, n1_norm, nm_norm, no_norm, nf_norm, ne_norm = (NormSemaphores(sem, n) for n in (
            "n1s", "n1", "nm", "no", "nf", "ne"))
        zo_squares, h2_squares, ff_squares = (SquareSemaphores(sem, n) for n in ("zo", "h2", "ff"))

        def due(count):
            return not isinstance(count, int) or count > 0

        def sb(name, shape, dt=f32):
            return ctx.enter_context(nc.sbuf_tensor(name, shape, dt))

        def region(name, nbytes, *phases):
            out = {}
            for tensors in phases:
                with ExitStack() as phase:
                    for n, shape, dt in tensors:
                        out[n] = phase.enter_context(nc.sbuf_tensor(n, shape, dt))
            ctx.enter_context(nc.sbuf_tensor(name, [P, nbytes], mybir.dt.uint8))
            return out

        KB = 1024
        r1 = region("operand_region", 64 * KB,
                    [("op_hi", [P, KT, SEQ], f32r), ("op_lo", [P, KT, SEQ], f32r)],
                    [("qq", [P, 2, SEQ], f32), ("kk", [P, 2, SEQ], f32), ("vv", [P, 2, NT, DH], f32),
                     ("sc", [P, QB, SEQ], f32), ("pr", [P, PR_W], f32), ("fb", [P, SEQ], f32),
                     ("lnc", [P, LNC_W], f32), ("ot", [P, 2, QB * P], f32)],
                    [("x2r", [P, KT, SEQ], f32), ("sq3", [P, 2, SEQ], f32), ("acc3", [P, SEQ], f32),
                     ("n3", [P, 2, SEQ], f32)])
        op_hi, op_lo = r1["op_hi"], r1["op_lo"]
        qq, kk, vv, sc, pr, fb, lnc, ot = (r1[n] for n in
            ("qq", "kk", "vv", "sc", "pr", "fb", "lnc", "ot"))
        r2 = region("hidden_region", 64 * KB,
                    [("ufh", [P, KT, UF], f32r), ("ufl", [P, KT, UF], f32r), ("vh", [P, 2, KT, VW], f32r),
                     ("vl", [P, 2, KT, VW], f32r), ("uf_raw", [P, KT, UF], f32), ("acc1", [P, SEQ], f32)],
                    [("dre", [P, NJ, TS + 1, CH], f32), ("dim", [P, NJ, TS + 1, CH], f32),
                     ("ere", [P, NJ, NC], f32), ("eim", [P, NJ, NC], f32), ("ut", [P, G, NC], f32),
                     ("tz", [P, G, P], f32), ("mt", [P, 2, NJ, P], f32), ("mb", [P, 2, NJ, P], f32),
                     ("pt", [P, 2, NJ, (TS + 1) * CH], f32), ("wg", [P, 2, SSM_W], f32),
                     ("row", [P, 2, SSM_W], f32)],
                    [("qa", [P, 2, SEQ], f32r), ("ql", [P, 2, SEQ], f32r), ("ks", [P, 2, SEQ], f32r),
                     ("vs", [P, 2, NT, P], f32r), ("pth", [P, 4, 2, QB * P], f32r),
                     ("ptl", [P, 4, 2, QB * P], f32r)],
                    [("x2", [P, KT, SEQ], f32), ("sq2", [P, 2, SEQ], f32), ("acc2", [P, SEQ], f32),
                     ("acc2b", [P, SEQ], f32), ("n2", [P, 2, SEQ], f32), ("sq2b", [P, 2, HALF], f32)],
                    [("hid_hi", [P, 8, SEQ], f32r), ("hid_lo", [P, 8, SEQ], f32r)])
        ufh, ufl, vh, vl, uf_raw, acc1 = (r2[n] for n in ("ufh", "ufl", "vh", "vl", "uf_raw", "acc1"))
        dre, dim_, ere, eim, ut, tz, mt, mb, pt, wg, row = (r2[n] for n in
            ("dre", "dim", "ere", "eim", "ut", "tz", "mt", "mb", "pt", "wg", "row"))
        qa, ql, ks, vs, pth, ptl = (r2[n] for n in ("qa", "ql", "ks", "vs", "pth", "ptl"))
        x2, sq2, acc2, acc2b, n2, sq2b = (r2[n] for n in ("x2", "sq2", "acc2", "acc2b", "n2", "sq2b"))
        hid_hi, hid_lo = r2["hid_hi"], r2["hid_lo"]
        r3 = region("sum_region", 32 * KB,
                    [("xt", [P, KT, SEQ], f32)],
                    [("vst", [P, NV, NT, VW], f32)],
                    [("hs", [P, 2, NJ, NC], f32), ("ss", [P, 2, NJ, NC], f32), ("qko", [P, 2, SEQ], f32),
                     ("yn", [P, TS, SSM_W], f32)],
                    [("skip_fz", [P, 24 * KB], mybir.dt.uint8), ("fz", [NH, 2, SEQ], f32)],
                    [("ya", [P, NT, 2 * NH, DH], f32)],
                    [("z", [P, KT, SEQ], f32)])
        xt, vst, hs, ss, qko, yn, fz, ya, z = (r3[n] for n in
            ("xt", "vst", "hs", "ss", "qko", "yn", "fz", "ya", "z"))
        r4 = region("chunk_region", 16 * KB,
                    [("w_hi", [P, 2, KT, P], f32r), ("w_lo", [P, 2, KT, P], f32r)],
                    [("sq1", [P, 2, SEQ], f32), ("n1", [P, 2, SEQ], f32)])
        w_hi, w_lo, sq1, n1 = (r4[n] for n in ("w_hi", "w_lo", "sq1", "n1"))
        w_raw = sb("w_raw", [P, 2, KT, P])
        r5 = region("small_region", 4 * TS * UF + 64,
                    [("ug", [P, G, TS, CH], f32), ("fl", [P, TS, NH], f32)],
                    [("tg", [P, SEQ], f32), ("hf", [P, SEQ], f32)])
        ug, fl, tg, hf = r5["ug"], r5["fl"], r5["tg"], r5["hf"]
        rb = sb("rb", [P, SEQ])
        g_sb = sb("g_sb", [P, 5, KT])
        ident = sb("ident", [P, P])
        ident2 = sb("ident2", [P, DH])
        ident_b = sb("ident_b", [P, P], bf16)
        mask_b = sb("mask_b", [P, QB, QB * P], bf16)
        ones = sb("ones", [P, P])
        sp = sb("sp", [P, 32, NJ])
        bc = sb("bc", [P, 4, NJ, CH])
        bbar = sb("bbar", [P, 2, NJ, CH])
        tb = sb("tb", [P, 2, NJ, CH])
        pw = sb("pw", [P, 2, TS + 1, NJ])
        rn = sb("rn", [P, 4, 2 * NT])
        nm = sb("nm", [P, UNITS, QB])
        den = sb("den", [P, UNITS, QB])
        rden = sb("rden", [P, 2, QB])
        wp = sb("wp", [P, 2, 8, NJ])
        ssy = sb("ssy", [P, 4, 3 * NT])
        bfs = sb("bfs", [NH, 1])

        ps = ctx.enter_context(nc.psum_tensor("ps", [P, 8, HALF], f32))

        LDT, AR, AI, DT, ARDT, TH, DEC, RHO, KR, RR, SN, SH, CS, ABR, ABI, M1, MAG, TA, TB_, CR, CI, PC, PSN, TC = range(24)
        WR, WI, T1, T2 = 24, 25, 26, 27

        def q(n):
            return sp[:, n, :]

        GAIN_PRE, GAIN_MIX, GAIN_POST, GAIN_FFN_PRE, GAIN_FFN_POST = range(5)

        op_hi_c = op_hi[:].rearrange("p k (c t) -> p k t c", t=TS)
        op_lo_c = op_lo[:].rearrange("p k (c t) -> p k t c", t=TS)
        kl = hs[:].rearrange("p r j c -> p (r j) c")
        gt = mt[:].rearrange("p r j c -> p (r j) c")
        sg = mb[:].rearrange("p r j c -> p (r j c)").rearrange("p (t n) -> p t n", t=TS)
        junk = pr[:, 0:NT * ATT_W].rearrange("p (m n) -> p m n", m=NT)
        ya_flat = ya[:].rearrange("p m h d -> p m (h d)")
        v_raw = w_raw[:].rearrange("p s k n -> p (s k n)").rearrange("p (k n) -> p k n", n=VW)

        def half(h):
            return slice(h * HALF, (h + 1) * HALF)

        def mix_view(op, k, h):
            if k < SSM_W // P:
                return (op_hi_c if op is op_hi else op_lo_c)[:, k, 4 * h:4 * h + 4, :]
            return op[:, k, half(h)]

        def mix_bank(k, n):
            bank = ps[:, 4 + n % 4, :]
            return bank.rearrange("p (t c) -> p t c", t=4) if k < SSM_W // P else bank

        block = ctx.enter_context(nc.Block())

        def ffn_bases():
            c, out = C_FFN, []
            for n in PARTS:
                out.append((c, c + 2 * n))
                c += 2 * n + KT
            return out, c

        BASES, C_END = ffn_bases()

        def steps(e, lo, hi, step, peel=0):
            for c in range(lo, lo + peel):
                step(c, c // 2, c % 2, c - lo)
            if hi > lo + peel:
                with e.Fori(0, (hi - lo - peel) // 2) as i:
                    for j in range(2):
                        step(i * 2 + (lo + peel + j), i + (lo + peel) // 2, j, i * 2 + (peel + j))

        def load_chunk(e, c, m, j, src, nk=KT):
            if due(c - 1):
                e.wait_ge(w_split, c - 1)
            e.dma_start(w_raw[:, j, 0:nk, :], src).then_inc(w_loaded[j], 16)

        def split_high(e, c, m, j):
            if due(c * 2 - 2):
                e.wait_ge(mm_done, c * 2 - 2)
            e.wait_ge(w_loaded[j], m * 16 + 16)
            e.activation(w_hi[:, j, :, :], w_raw[:, j, :, :], ACT.Copy).then_inc(w_high, 1)

        def split_low(e, c, m, j):
            e.wait_ge(w_high, c + 1)
            e.tensor_tensor(w_lo[:, j, :, :], w_raw[:, j, :, :], w_hi[:, j, :, :].bitcast(f32),
                            ALU.subtract).then_inc(w_split, 1)

        def ahead(split, e, c, m, j):
            split(e, c + 1, m + j, 1 - j)

        def chunk_products(e, c, j, x_hi, x_lo, nk=KT, before=None):
            e.wait_ge(w_split, c + 1)
            for h in range(2):
                if due(c * 2 + (h - 3)):
                    e.wait_ge(evacuated, c * 2 + (h - 3))
                out = ps[:, 2 * j + h, :]
                for k in range(nk):
                    if before:
                        before(h, k)
                    e.matmul(out, w_hi[:, j, k, :], x_hi[:, k, half(h)], start=k == 0, stop=False)
                    e.matmul(out, w_hi[:, j, k, :], x_lo[:, k, half(h)], start=False, stop=False)
                    last = e.matmul(out, w_lo[:, j, k, :], x_hi[:, k, half(h)], start=False, stop=k == nk - 1)
                last.then_inc(mm_done, 1)

        def norm_sums(e, norm, acc, bank, h):
            e.matmul(ps[:, bank + h, :], ones[:], acc[:, half(h)], start=True,
                     stop=True).then_inc(norm.sums, 1)

        def rsqrt_in(e, norm, v, sums, n):
            e.tensor_scalar(v, sums, 1.0 / n, EPS, ALU.mult, ALU.add).then_inc(norm.mean, 1)

        def rsqrt_act(e, norm, y, v, count=1):
            e.wait_ge(norm.mean, count)
            e.activation(y, v, ACT.Ln).then_inc(norm.ln, 1)
            e.wait_ge(norm.ln, count)
            e.activation(y, y, ACT.Exp, scale=-0.5).then_inc(norm.seed, 1)

        def rsqrt_out(e, link, norm, y, v, t, count=1):
            e.wait_ge(norm.seed, count)
            link(e.tensor_tensor(t, y, y, ALU.mult))
            link(e.tensor_tensor(t, t, v, ALU.mult))
            link(e.tensor_scalar(t, t, -0.5, 1.5, ALU.mult, ALU.add))
            e.tensor_tensor(y, y, t, ALU.mult).then_inc(norm.rstd, 1)

        @block.sync
        def _(sync):
            sync.dma_start(sp[:, 0:3, :], s_par).then_inc(par_in, 16)
            sync.dma_start(bc[:], s_bc).then_inc(par_in, 16)
            sync.dma_start(g_sb[:], gains).then_inc(gains_in, 16)
            for k in range(KT):
                sync.dma_start(xt[:, k, :], x_t[:, k, :]).then_inc(x_in[k], 16)
                if k in (1, 3):
                    a = 4 * (k // 2)
                    sync.dma_start(uf_raw[:, a:a + 4, :], w_uf[:, a:a + 4, :]).then_inc(uf_in[k // 2], 16)
            sync.dma_start(bfs[:], b_f).then_inc(bf_in, 16)
            for w in range(NV):
                if due(w):
                    sync.wait_ge(v_split, w)
                sync.dma_start(v_raw, w_v[w]).then_inc(v_in, 16)
            sync.wait_ge(v_split, NV)
            for j in range(2):
                load_chunk(sync, j, 0, j, w_stream[j])
            for w in range(NV):
                sync.wait_ge(v_scaled, NT * (w + 1))
                for h in range(4):
                    sync.dma_start(v_dram[4 * w + h], vst[:, w, :, h * DH:(h + 1) * DH]).then_inc(v_out, 16)

            for part in range(NH // 2):
                with sync.Fori(0, 2) as i:
                    for j in range(2):
                        c = i * 2 + (4 * part + j)
                        sync.wait_ge(w_split, c + 1)
                        sync.dma_start(w_raw[:, j, :, :], w_stream[c + 2]).then_inc(w_loaded[j], 16)
                        sync.wait_ge(evacuated, c * 2 + 2)
                        sync.dma_start(qk_dram[i * 2 + j, part], qko[:, j, :]).then_inc(qk_out[j], 16)

            sync.wait_ge(mm_done, 2 * C_OUT)
            sync.dma_start(lnc[:], lnc_dram).then_inc(lnc_in, 16)
            for j in range(2):
                sync.wait_ge(qk_out[j], 16 * NH)
            sync.wait_ge(v_out, 16 * 4 * NV)
            sync.wait_ge(cum_out, 16)

            def stage(i, j, hc):
                if due(hc * 3 - 3):
                    sync.wait_ge(low_parts_done, hc * 3 - 3)
                for half in range(2):
                    r = slice(half * DH, (half + 1) * DH)
                    sync.dma_start(qq[r, j, :], qk_heads[2 * j, i]).then_inc(staged[j], 16)
                    sync.dma_start(kk[r, j, :], qk_heads[2 * j + 1, i]).then_inc(staged[j], 16)
                sync.dma_start(vv[:, j, :, :], v_dram[i + NH * j]).then_inc(staged[j], 16)
                if j == 1:
                    if due(hc * NT - NT):
                        sync.wait_ge(row_max_done, hc * NT - NT)
                    sync.dma_start(fb[:], cum_dram[i].partition_broadcast(P)).then_inc(fb_in, 16)

            for i in range(2):
                for j in range(2):
                    stage(i, j, 2 * i + j)
            with sync.Fori(2, NH) as i:
                for j in range(2):
                    stage(i, j, i * 2 + j)

            sync.wait_ge(pv_done, 2 * NH * 10)
            for k in range(KT):
                sync.dma_start(x2[:, k, :], x_t[:, k, :]).then_inc(x_again[k], 16)
            with sync.Fori(0, KT // 2) as i:
                for j in range(2):
                    c = i * 2 + (C_OUT + 2 + j)
                    load_chunk(sync, c, i + (C_OUT + 2) // 2, j, w_stream[c])
            sync.wait_ge(x2_done, 2 * KT)
            sync.dma_start(x2_dram, x2[:]).then_inc(x2_out, 16)
            first, last = C_FFN + 2, BASES[-1][1]
            with sync.Fori(0, (last - first) // 2) as i:
                for j in range(2):
                    c = i * 2 + (first + j)
                    load_chunk(sync, c, i + first // 2, j, w_stream[c])
            for c in range(KT):
                load_chunk(sync, last + c, (last + c) // 2, c % 2, w_last[c], PARTS[-1])
                if c == 1:
                    sync.wait_ge(x2_out, 16)
                    sync.wait_ge(mm_done, 2 * last)
                    sync.dma_start(r1["x2r"][:], x2_dram).then_inc(x2_again, 16)
            for h in range(2):
                for k in range(KT):
                    sync.wait_ge(out_done, h * KT + k + 1)
                    tok = slice(h * HALF, (h + 1) * HALF)
                    sync.dma_start(out_t[:, k, tok], z[:, k, tok]).then_inc(out_stored, 16)
            sync.wait_ge(out_stored, 16 * 2 * KT)

        def quarter(a):
            return ps[:, 4 + a, :].rearrange("p (g c) -> p g c", g=4)

        def group_at(a, b):
            return 2 * (4 * (a % 2) + b) + a // 2

        def bank_of(g):
            return 2 * (g % 2) + g // 8, g // 2 % 4

        def slot_of(j, g, b):
            return 10 * j + g * (g + 1) // 2 + b

        BODY = [(j, g) for j in range(2) for g in ORDER]
        PIECES = [(j, g, b) for j, g in BODY for b in range(g + 1)]

        def piece(i, j, g, b):
            return i * (2 * PCS) + slot_of(j, g, b)

        def slot_of(j, g, b):
            return j * PCS + sum(f + 1 for f in ORDER[:PLACE[g]]) + b

        def unit(i, j, g):
            return i * (2 * UNITS) + (j * UNITS + PLACE[g])

        def shifted(seq, i, n, by, last):
            n += by
            if n >= len(seq):
                return None if last else (i + 1, *seq[n - len(seq)])
            return (i, *seq[n])

        def bodies(e, step):
            def body(i, first, last):
                for n, (j, g) in enumerate(BODY):
                    prev = (i, *BODY[n - 1]) if n else (None if first else (i - 1, *BODY[-1]))
                    on = [shifted(PIECES, i, slot_of(j, g, b), 2, last) for b in range(g + 1)]
                    step(i, j, g, shifted(BODY, i, n, 2, last), prev, on, last)
            body(0, True, False)
            with e.Fori(1, NH - 1) as i:
                body(i, False, False)
            body(NH - 1, False, True)

        def probs(g, r):
            w = (g + 1) * QB * P
            at = QB * QB * P * g * (g + 1) // 2 + r * w
            return pr[:, at:at + w]

        def outputs_bank(g):
            return ps[:, 6 + PLACE[g] % 2, 0:QB * P]

        def y_bank(g, r):
            return ps[:, 6 + PLACE[g] % 2, QB * P + r * DH:QB * P + (r + 1) * DH]

        @block.scalar
        def _(act):
            act.wait_ge(par_in, 32)
            act.activation(q(DT), q(LDT), ACT.Exp).then_inc(par_act, 1)
            act.wait_ge(par_dve, 1)
            act.activation(q(DEC), q(ARDT), ACT.Exp)
            act.activation(q(RHO), q(ARDT), ACT.Exp, scale=float(TS)).then_inc(par_act, 1)
            act.wait_ge(par_dve, 2)
            act.activation(q(SN), q(RR), ACT.Sin)
            act.activation(q(SH), q(RR), ACT.Sin, scale=0.5).then_inc(par_act, 1)

            act.wait_ge(gains_in, 16)
            for k in range(KT):
                act.wait_ge(x_in[k], 16)
                act.activation(op_hi[:, k, :], xt[:, k, :], ACT.Copy,
                               scale=g_sb[:, GAIN_PRE, k:k + 1]).then_inc(x_high, 1)
                if due(k - 1):
                    act.wait_ge(sq_added, k - 1)
                act.activation(sq1[:, k % 2, :], xt[:, k, :], ACT.Square).then_inc(sq_x, 1)
                if k in (1, 3):
                    a = 4 * (k // 2)
                    act.wait_ge(uf_in[k // 2], 16)
                    act.activation(ufh[:, a:a + 4, :], uf_raw[:, a:a + 4, :], ACT.Copy).then_inc(uf_high, 1)

            def v_high(w):
                act.wait_ge(v_in, 16 * (w + 1))
                if due(NT * (w - 1)):
                    act.wait_ge(v_mm, NT * (w - 1))
                act.activation(vh[:, w % 2, :, :], v_raw, ACT.Copy).then_inc(v_high_done, 1)

            v_high(0)
            act.wait_ge(uf_mm, 1)
            for s in range(TS):
                act.activation(ug[:, :, s, :], ps[:, s, 0:SSM_W].rearrange("p (g c) -> p g c", c=CH), ACT.Copy)
            ins = act.activation(fl[:], ps[:, :, SSM_W:UF], ACT.Copy)
            ins.then_inc(uf_copied, 1)
            rsqrt_act(act, n1s_norm, rn[:, 0, :], rn[:, 1, :])
            rsqrt_act(act, n1_norm, rb[:], n1[:, 0, :])
            act.wait_ge(n1s_norm.rstd, 1)
            act.wait_ge(x_split, KT)
            for w in range(NV):
                if w + 1 < NV:
                    v_high(w + 1)
                for m in range(NT):
                    act.wait_ge(v_mm, NT * w + m + 1)
                    act.activation(vst[:, w, m, :], ps[:, 4 + m % 4, 0:VW], ACT.Copy,
                                   scale=rn[:, 0, m:m + 1]).then_inc(v_scaled, 1)
            act.wait_ge(n1_norm.rstd, 1)
            split_high(act, 0, 0, 0)
            act.wait_ge(f_abs, 1)
            act.activation(fz[:, 1, :], fz[:, 1, :], ACT.Exp).then_inc(f_exp, 1)
            act.wait_ge(f_exp, 1)
            act.activation(fz[:, 1, :], fz[:, 1, :], ACT.Ln, bias=ones[0:NH, 0:1]).then_inc(f_ln, 1)
            for a in range(4):
                act.wait_ge(ut_mm, a + 1)
                ins = act.activation(ut[:, 4 * a:4 * a + 4, :], quarter(a), ACT.Copy)
            ins.then_inc(ut_out, 1)

            def qk_step(c, m, j, n):
                ahead(split_high, act, c, m, j)

            steps(act, 0, 4, qk_step, peel=4)
            for a in range(4):
                act.wait_ge(mb_mm, a + 1)
                ins = act.activation(mb[:, a // 2, 4 * (a % 2):4 * (a % 2) + 4, :], quarter(a), ACT.Copy)
            ins.then_inc(mb_out, 1)
            for a in range(4):
                act.wait_ge(kl_mm, a + 1)
                ins = act.activation(kl[0:CH, group_at(a, 0):group_at(a, 3) + 1:2, :],
                                     ps[0:CH, 4 + a, :].rearrange("p (g c) -> p g c", g=4), ACT.Copy)
            ins.then_inc(kl_out, 1)
            steps(act, 4, 8, qk_step)
            act.wait_ge(y_sum, 1)
            act.activation(yn[:], yn[:], ACT.Gelu_apprx_tanh).then_inc(gelu_done, 1)
            steps(act, 8, 12, qk_step)
            for a in range(4):
                act.wait_ge(gt_mm, a + 1)
                ins = act.activation(gt[:, 4 * a:4 * a + 4, :], quarter(a), ACT.Copy)
            ins.then_inc(gt_out, 1)
            act.wait_ge(glu_sum, 1)
            act.activation(sg[:], sg[:], ACT.Sigmoid).then_inc(glu_sig, 1)
            act.wait_ge(y_gated, 1)
            for t in range(TS):
                ins = act.activation(sg[:, t, :], yn[:, t, :], ACT.Square, accum_out=ssy[:, 0, t:t + 1])
            ins.then_inc(y_ssm_sq, 1)

            def exp_row(i, j, g, r):
                u = unit(i, j, g)
                if due(piece(i, j, g, 0) - (PCS - g - 1)):
                    act.wait_ge(pt_mm, piece(i, j, g, 0) - (PCS - g - 1))
                if due(u - 3):
                    act.wait_ge(y_done, u - 3)
                act.wait_ge(row_max_done, u * 2 + (r + 1))
                act.activation(probs(g, r), sc[:, r, 0:(g + 1) * QB * P], ACT.Exp, scale=-1.0,
                               bias=nm[:, g, r:r + 1], accum_out=den[:, g, r:r + 1]).then_inc(exp_done, 1)

            def pt_high(i, j, g, b):
                pc, slot = piece(i, j, g, b), slot_of(j, g, b)
                if due(pc - 3):
                    act.wait_ge(pv_done, pc - 3)
                act.wait_ge(pt_mm, pc + 1)
                act.activation(pth[:, slot % 4, :, :], ps[:, 4 + slot % 2, :].rearrange("p (b n) -> p b n", b=2),
                               ACT.Copy).then_inc(pt_high_done, 1)

            def ot_copy(i, j, g):
                if due(unit(i, j, g) - 1):
                    act.wait_ge(yt_mm, unit(i, j, g) - 1)
                act.wait_ge(pv_done, piece(i, j, g, g) + 1)
                act.activation(ot[:, PLACE[g] % 2, :], outputs_bank(g), ACT.Copy).then_inc(ot_done, 1)

            def act_unit(i, j, g, ahead_, prev, on, last):
                if prev:
                    ot_copy(*prev)
                for b in range(max(g + 1, 2)):
                    if b < len(on) and on[b]:
                        pt_high(*on[b])
                    if b < QB and ahead_:
                        exp_row(*ahead_, b)

            for g in ORDER[:2]:
                for r in range(QB):
                    exp_row(0, 0, g, r)
            for n in range(2):
                pt_high(0, *PIECES[n])
            bodies(act, act_unit)
            ot_copy(NH - 1, *BODY[-1])

            act.wait_ge(y_done, 2 * NH * UNITS)
            for a in range(2):
                for m in range(NT):
                    s = (a + 1) * NT + m
                    if due(a * NT + m - 7):
                        act.wait_ge(y_att_sq, a * NT + m - 7)
                    act.activation(junk[:, m, 0:ATT_W], ya_flat[:, m, a * ATT_W:(a + 1) * ATT_W], ACT.Square,
                                   accum_out=ssy[:, 0, s:s + 1]).then_inc(y_att_sq, 1)
            rsqrt_act(act, nm_norm, ssy[:, 2, :], ssy[:, 1, :])
            act.wait_ge(nm_norm.rstd, 1)
            for m in range(NT):
                part = ya_flat[:, m, ATT_W:2 * ATT_W]
                ins = act.activation(part, part, ACT.Copy, scale=ssy[:, 2, 2 * NT + m:2 * NT + m + 1])
            ins.then_inc(fox_scaled, 1)
            for n in range(2 * KT):
                k, h = n // 2, n % 2
                act.wait_ge(mix_mm, n + 1)
                act.activation(mix_view(op_hi, k, h), mix_bank(k, n), ACT.Copy,
                               scale=g_sb[:, GAIN_MIX, k:k + 1]).then_inc(mix_high, 1)

            def z_square(squares, sq):
                def step(c, m, j, n):
                    ahead(split_high, act, c, m, j)
                    if due(n - 1):
                        act.wait_ge(squares.added, n - 1)
                    act.wait_ge(evacuated, c * 2 + 2)
                    act.wait_ge(gains_in, 16)
                    act.activation(sq[:, j, :], z[:, n, :], ACT.Square).then_inc(squares.sq, 1)
                return step

            steps(act, C_OUT, C_OUT + KT, z_square(zo_squares, sq2), peel=2)
            for h in range(2):
                rsqrt_act(act, no_norm, rb[:, half(h)], n2[:, 0, half(h)], h + 1)
            for h in range(2):
                for k in range(KT):
                    n = h * KT + k
                    act.wait_ge(x2_done, n + 1)
                    act.activation(op_hi[:, k, half(h)], x2[:, k, half(h)], ACT.Copy,
                                   scale=g_sb[:, GAIN_FFN_PRE, k:k + 1]).then_inc(h2_high, 1)
                    if due(n - 1):
                        act.wait_ge(h2_squares.added, n - 1)
                    act.activation(sq2b[:, n % 2, :], x2[:, k, half(h)], ACT.Square).then_inc(h2_squares.sq, 1)
            for h in range(2):
                rsqrt_act(act, nf_norm, rb[:, half(h)], n2[:, 0, half(h)], h + 1)

            def gate_up(m0, f0):
                def step(c, m, j, n):
                    ahead(split_high, act, c, m, j)
                    f = m - (m0 - f0)
                    for h in range(2):
                        if j == 0:
                            act.wait_ge(evacuated, c * 2 + (h + 1))
                            act.activation(tg[:, half(h)], tg[:, half(h)], ACT.Silu).then_inc(silu_done, 1)
                        else:
                            act.wait_ge(hf_done, f * 2 + (h + 1))
                            act.wait_ge(x2_out, 16)
                            act.activation(hid_hi[:, m - m0, half(h)], hf[:, half(h)],
                                           ACT.Copy).then_inc(hid_high, 1)
                return step

            for p_ in range(len(PARTS)):
                gu, dn = BASES[p_]
                steps(act, gu, dn, gate_up(gu // 2, sum(PARTS[:p_])))
                if p_ < len(PARTS) - 1:
                    steps(act, dn, dn + KT, qk_step)
                else:
                    last = z_square(ff_squares, r1["sq3"])
                    steps(act, dn, dn + KT - 2, last, peel=2)
                    last(dn + KT - 2, (dn + KT - 2) // 2, 0, KT - 2)
                    act.wait_ge(ff_squares.added, KT - 2)
                    act.wait_ge(evacuated, 2 * C_END)
                    act.activation(r1["sq3"][:, 1, :], z[:, KT - 1, :], ACT.Square).then_inc(ff_squares.sq, 1)
            for h in range(2):
                rsqrt_act(act, ne_norm, rb[:, half(h)], r1["n3"][:, 0, half(h)], h + 1)

        @block.vector
        def _(dve):
            chain = [0]

            def link(ins):
                chain[0] += 1
                ins.then_inc(dve_chain, 1)
                dve.wait_ge(dve_chain, chain[0])

            def tt(out, a, b, op):
                return dve.tensor_tensor(out, a, b, op)

            def cmul(o_re, o_im, a_re, a_im, b_re, b_im, t1, t2):
                tt(t1, a_re, b_re, ALU.mult)
                link(tt(t2, a_im, b_im, ALU.mult))
                link(tt(o_re, t1, t2, ALU.subtract))
                tt(t1, a_re, b_im, ALU.mult)
                link(tt(t2, a_im, b_re, ALU.mult))
                link(tt(o_im, t1, t2, ALU.add))

            dve.memset(ones[:], 1.0).then_inc(ones_set, 1)
            dve.wait_ge(par_act, 1)
            link(tt(q(ARDT), q(AR), q(DT), ALU.mult))
            tt(q(TH), q(AI), q(DT), ALU.mult).then_inc(par_dve, 1)
            dve.wait_ge(par_dve, 1)
            magic = 12582912.0
            link(dve.tensor_scalar(q(KR), q(TH), 1.0 / (2 * math.pi), magic, ALU.mult, ALU.add))
            link(dve.tensor_scalar(q(KR), q(KR), magic, None, ALU.subtract))
            c1 = 6.28125
            c2 = float((np.float32(2 * math.pi - c1).view(np.uint32) & np.uint32(0xFFFFE000)).view(np.float32))
            c3 = 2 * math.pi - c1 - c2
            link(dve.scalar_tensor_tensor(out=q(RR), in0=q(KR), scalar=-c1, in1=q(TH), op0=ALU.mult, op1=ALU.add))
            link(dve.scalar_tensor_tensor(out=q(RR), in0=q(KR), scalar=-c2, in1=q(RR), op0=ALU.mult, op1=ALU.add))
            link(dve.scalar_tensor_tensor(out=q(RR), in0=q(KR), scalar=-c3, in1=q(RR), op0=ALU.mult, op1=ALU.add))
            pi = 3.1415925
            dve.tensor_scalar(q(RR), q(RR), pi, -pi, ALU.min, ALU.max).then_inc(par_dve, 1)
            dve.wait_ge(par_act, 3)
            link(tt(q(CS), q(SH), q(SH), ALU.mult))
            link(dve.tensor_scalar(q(CS), q(CS), -2.0, 1.0, ALU.mult, ALU.add))
            link(tt(q(ABR), q(DEC), q(CS), ALU.mult))
            link(tt(q(ABI), q(DEC), q(SN), ALU.mult))
            dve.tensor_scalar(q(M1), q(ABR), -1.0, None, ALU.add)
            tt(q(MAG), q(AR), q(AR), ALU.mult)
            link(tt(q(TA), q(AI), q(AI), ALU.mult))
            link(tt(q(MAG), q(MAG), q(TA), ALU.add))
            link(dve.reciprocal(q(MAG), q(MAG)))
            tt(q(CR), q(M1), q(AR), ALU.mult)
            link(tt(q(TA), q(ABI), q(AI), ALU.mult))
            link(tt(q(CR), q(CR), q(TA), ALU.add))
            link(tt(q(CR), q(CR), q(MAG), ALU.mult))
            tt(q(CI), q(ABI), q(AR), ALU.mult)
            link(tt(q(TA), q(M1), q(AI), ALU.mult))
            link(tt(q(CI), q(CI), q(TA), ALU.subtract))
            link(tt(q(CI), q(CI), q(MAG), ALU.mult))
            cr = q(CR).unsqueeze(2).to_broadcast((P, NJ, CH))
            ci = q(CI).unsqueeze(2).to_broadcast((P, NJ, CH))
            cmul(bbar[:, 0], bbar[:, 1], cr, ci, bc[:, 0], bc[:, 1], tb[:, 0], tb[:, 1])
            dve.tensor_scalar(tb[:, 0], bc[:, 2], -1.0, None, ALU.mult)
            dve.tensor_scalar(tb[:, 1], bc[:, 3], -1.0, None, ALU.mult)
            dve.memset(pw[:, 0, 0, :], 1.0)
            dve.memset(pw[:, 1, 0, :], 0.0)
            dve.tensor_copy(pw[:, 0, 1, :], q(ABR))
            link(dve.tensor_copy(pw[:, 1, 1, :], q(ABI)))
            n = 1
            while n < TS:
                hi = slice(n + 1, 2 * n + 1)
                lo = slice(1, n + 1)
                a_re, a_im = (pw[:, r, lo, :] for r in range(2))
                b_re, b_im = (pw[:, r, n:n + 1, :].to_broadcast((P, n, NJ)) for r in range(2))
                t1 = n1[:, 0, 0:n * NJ].rearrange("p (l j) -> p l j", j=NJ)
                t2 = n1[:, 1, 0:n * NJ].rearrange("p (l j) -> p l j", j=NJ)
                cmul(pw[:, 0, hi, :], pw[:, 1, hi, :], a_re, a_im, b_re, b_im, t1, t2)
                n *= 2
            dve.tensor_copy(wp[:, 0, 7, :], q(CS))
            link(dve.tensor_copy(wp[:, 1, 7, :], q(SN)))
            src = 7
            squarings = [7, 7, 0] + list(range(1, 7))
            for dst in squarings:
                cmul(q(T1), q(T2), wp[:, 0, src], wp[:, 1, src], wp[:, 0, src], wp[:, 1, src], q(TA), q(TB_))
                dve.tensor_copy(wp[:, 0, dst, :], q(T1))
                link(dve.tensor_copy(wp[:, 1, dst, :], q(T2)))
                src = dst
            dve.tensor_copy(q(TC), q(T1)).then_inc(powers, 1)

            dve.wait_ge(gains_in, 16)
            for k in range(KT):
                dve.wait_ge(x_high, k + 1)
                dve.scalar_tensor_tensor(out=op_lo[:, k, :], in0=xt[:, k, :], scalar=g_sb[:, GAIN_PRE, k:k + 1],
                                         in1=op_hi[:, k, :].bitcast(f32), op0=ALU.mult,
                                         op1=ALU.subtract).then_inc(x_split, 1)
                if k in (1, 3):
                    a = 4 * (k // 2)
                    dve.wait_ge(uf_high, k // 2 + 1)
                    tt(ufl[:, a:a + 4, :], uf_raw[:, a:a + 4, :], ufh[:, a:a + 4, :].bitcast(f32),
                       ALU.subtract).then_inc(uf_split, 1)

            def v_low(w):
                dve.wait_ge(v_high_done, w + 1)
                tt(vl[:, w % 2, :, :], v_raw, vh[:, w % 2, :, :].bitcast(f32), ALU.subtract).then_inc(v_split, 1)

            v_low(0)
            dve.wait_ge(n1s_norm.sums, 1)
            rsqrt_in(dve, n1s_norm, rn[:, 1, :], ps[:, 2, 0:2 * NT], D)
            rsqrt_out(dve, link, n1s_norm, rn[:, 0, :], rn[:, 1, :], rn[:, 2, :])
            dve.wait_ge(n1_norm.sums, 2)
            rsqrt_in(dve, n1_norm, n1[:, 0, :], ps[:, 0:2, :].rearrange("p b n -> p (b n)"), D)
            rsqrt_out(dve, link, n1_norm, rb[:], n1[:, 0, :], n1[:, 1, :])
            v_low(1)
            v_low(2)
            dve.wait_ge(n1s_norm.rstd, 1)
            dve.wait_ge(uf_copied, 1)
            rs = rn[:, 0, NT:2 * NT]
            tt(fl[:], fl[:], rs.unsqueeze(2).to_broadcast((P, TS, NH)), ALU.mult)
            tt(ug[:], ug[:], rs.unsqueeze(1).unsqueeze(3).to_broadcast((P, G, TS, CH)),
               ALU.mult).then_inc(uf_scaled, 1)
            split_low(dve, 0, 0, 0)
            dve.wait_ge(f_mm, 1)
            dve.wait_ge(bf_in, 16)
            f_in = ps[0:NH, 2:4, :].rearrange("p b n -> p (b n)").rearrange("p (s c) -> p c s", s=TS)
            link(dve.tensor_scalar(fz[:, 0, :].rearrange("p (c s) -> p c s", s=TS), f_in, bfs[:, 0:1], None, ALU.add))
            dve.scalar_tensor_tensor(out=fz[:, 1, :], in0=fz[:, 0, :], scalar=-1.0, in1=fz[:, 0, :], op0=ALU.mult,
                                     op1=ALU.min).then_inc(f_abs, 1)
            dve.wait_ge(v_out, 16 * 4 * NV)
            dve.wait_ge(v_mm, NV * NT)
            shape = (P, NJ, TS, CH)
            a_re, a_im = (pw[:, r, 0:TS, :].rearrange("p l j -> p j l").unsqueeze(3).to_broadcast(shape) for r in range(2))
            b_re, b_im = (bbar[:, r].unsqueeze(2).to_broadcast(shape) for r in range(2))
            m_re, m_im = (mt[:, r].rearrange("p j (s c) -> p j s c", s=TS) for r in range(2))
            u1, u2 = (hs[:, r].rearrange("p j (s c) -> p j s c", s=TS) for r in range(2))
            for s in range(TS):
                l_ = TS - 1 - s
                cmul(m_re[:, :, s], m_im[:, :, s], a_re[:, :, l_], a_im[:, :, l_], b_re[:, :, 0], b_im[:, :, 0],
                     u1[:, :, s], u2[:, :, s])
            dve.tensor_copy(q(TC), q(T1)).then_inc(mt_done, 1)
            dve.wait_ge(f_ln, 1)
            link(dve.tensor_scalar(fz[:, 0, :], fz[:, 0, :], 0.0, None, ALU.min))
            link(tt(fz[:, 1, :], fz[:, 1, :], fz[:, 0, :], ALU.subtract))
            dve.tensor_tensor_scan(out=fz[:, 0, :], data0=ones[0:NH, 0:1].to_broadcast((NH, SEQ)), data1=fz[:, 1, :],
                                   initial=0.0, op0=ALU.mult, op1=ALU.add).then_inc(f_cum, 1)

            def qk_step(c, m, j, n):
                ahead(split_low, dve, c, m, j)
                if due(m * 16):
                    dve.wait_ge(qk_out[j], m * 16)
                for h in range(2):
                    dve.wait_ge(mm_done, c * 2 + (h + 1))
                    dve.scalar_tensor_tensor(out=qko[:, j, half(h)], in0=ps[:, 2 * j + h, :],
                                             scalar=DH ** -0.5 if j == 0 else 1.0, in1=rb[:, half(h)],
                                             op0=ALU.mult, op1=ALU.mult).then_inc(evacuated, 1)

            steps(dve, 0, 4, qk_step, peel=4)
            dve.wait_ge(x_mm, 1)
            dve.wait_ge(e_done, 1)
            x_re, x_im = (ps[:, 4 + 2 * r:6 + 2 * r, :].rearrange("p b (j c) -> p (b j) c", c=NC) for r in range(2))
            t1, t2 = (pt[:, r, :, 0:NC] for r in range(2))
            z_re, z_im = mt[:, 0], mt[:, 1]
            tt(t1, x_re, ere[:], ALU.mult)
            link(tt(t2, x_im, eim[:], ALU.mult))
            link(tt(z_re, t1, t2, ALU.add))
            tt(t1, x_im, ere[:], ALU.mult)
            link(tt(t2, x_re, eim[:], ALU.mult))
            link(tt(z_im, t1, t2, ALU.subtract))
            for r in range(2):
                for j in range(NJ):
                    ins = dve.tensor_tensor_scan(out=ss[:, r, j, :], data0=sp[:, RHO, j:j + 1].to_broadcast((P, NC)),
                                                 data1=mt[:, r, j, :], initial=0.0, op0=ALU.mult, op1=ALU.add)
            link(ins)
            dve.wait_ge(tz_in, 16 * TS)
            dve.memset(hs[:, :, :, 0:1], 0.0)
            cut = slice(0, NC - 1)
            cmul(hs[:, 0, :, 1:NC], hs[:, 1, :, 1:NC], ss[:, 0, :, cut], ss[:, 1, :, cut],
                 ere[:, :, cut], eim[:, :, cut], t1[:, :, cut], t2[:, :, cut])
            dve.tensor_copy(q(TC), q(T1)).then_inc(h_done, 1)
            steps(dve, 4, 8, qk_step)
            dve.wait_ge(y_mm, 1)
            dve.wait_ge(du_done, 1)
            for g in range(G):
                a, b = bank_of(g)
                y = ps[:, 4 + a, b * P:(b + 1) * P].rearrange("p (t o) -> p t o", t=TS)
                ins = tt(yn[:, :, g * CH:(g + 1) * CH], y, ug[:, g], ALU.add)
            ins.then_inc(y_sum, 1)
            steps(dve, 8, 12, qk_step)
            dve.wait_ge(glu_mm, 1)
            tt(sg[:], ps[:, 4:8, :].rearrange("p b (t n) -> p (b t) n", t=2),
               row[:, 1:2, :].to_broadcast((P, TS, SSM_W)), ALU.add).then_inc(glu_sum, 1)
            dve.wait_ge(glu_sig, 1)
            tt(yn[:], yn[:], sg[:], ALU.mult).then_inc(y_gated, 1)

            dve.wait_ge(y_ssm_sq, 1)
            for j in range(2):
                dve.wait_ge(qk_out[j], 16 * NH)

            def qk_high(i, j):
                hc = i * 2 + j
                if due(hc * NT - NT):
                    dve.wait_ge(qk_done, hc * NT - NT)
                dve.wait_ge(staged[j], i * 80 + 80)
                dve.tensor_copy(qa[:, j, :], qq[:, j, :])
                dve.tensor_copy(ks[:, j, :], kk[:, j, :]).then_inc(qk_high_done, 1)

            def values_high(i, j):
                hc = i * 2 + j
                if due(hc * PCS - PCS):
                    dve.wait_ge(pv_done, hc * PCS - PCS)
                dve.wait_ge(staged[j], i * 80 + 80)
                dve.tensor_copy(vs[:, j, :, 0:DH], vv[:, j, :, :]).then_inc(values_high_done, 1)

            def row_max(i, j, g, r):
                u, w = unit(i, j, g), (g + 1) * QB * P
                dve.wait_ge(qk_done, u * 2 + (r + 1))
                if due(u * 2 + (r - 1)):
                    dve.wait_ge(exp_done, u * 2 + (r - 1))
                if j == 0:
                    off = SEQ - P - P * (QB * g + r)
                    bias = lnc[:, off:off + w]
                else:
                    dve.wait_ge(fb_in, i * 16 + 16)
                    bias = fb[:, 0:w]
                dve.wait_ge(lnc_in, 16)
                dve.sem_inc(dve_waited, 1)
                dve.tensor_tensor_reduce(out=sc[:, r, 0:w], in0=ps[:, 2 * r:2 * r + 2, :].rearrange("p b n -> p (b n)")[:, 0:w],
                                         in1=bias, scale=-1.0, scalar=3e38, op0=ALU.add, op1=ALU.min,
                                         accum_out=nm[:, g, r:r + 1]).then_inc(row_max_done, 1)

            def pt_low(i, j, g, b):
                pc, slot = piece(i, j, g, b), slot_of(j, g, b)
                dve.wait_ge(pt_high_done, pc + 1)
                tt(ptl[:, slot % 4, :, :], ps[:, 4 + slot % 2, :].rearrange("p (b n) -> p b n", b=2),
                   pth[:, slot % 4, :, :].bitcast(f32), ALU.subtract).then_inc(pt_low_done, 1)

            def y_unit(i, j, g):
                u = unit(i, j, g)
                dve.wait_ge(yt_mm, u + 1)
                dve.reciprocal(rden[:, PLACE[g] % 2, :], den[:, g, :]).then_inc(rden_done, 1)
                dve.wait_ge(rden_done, u + 1)
                tt(ya[:, QB * g:QB * (g + 1), i + NH * j, :],
                   ps[:, 6 + PLACE[g] % 2, QB * P:QB * P + QB * DH].rearrange("p (r d) -> p r d", r=QB),
                   rden[:, PLACE[g] % 2, :].unsqueeze(2).to_broadcast((P, QB, DH)), ALU.mult).then_inc(y_done, 1)

            def dve_unit(i, j, g, ahead_, prev, on, last):
                for b in range(max(g + 1, 2)):
                    if b < QB and ahead_:
                        row_max(*ahead_, b)
                    if b < len(on) and on[b]:
                        pt_low(*on[b])
                    if b == 1 and prev:
                        y_unit(*prev)
                if g == ORDER[-1] and not last:
                    qk_high(i + 1, j)
                if g == ORDER[0] and not (last and j == 1):
                    values_high(*((i, 1) if j == 0 else (i + 1, 0)))

            qk_high(0, 0)
            values_high(0, 0)
            qk_high(0, 1)
            for g in ORDER[:2]:
                for r in range(QB):
                    row_max(0, 0, g, r)
            for n in range(2):
                pt_low(0, *PIECES[n])
            bodies(dve, dve_unit)
            y_unit(NH - 1, *BODY[-1])

            dve.wait_ge(y_att_sq, 2 * NT)
            dve.tensor_scalar(ssy[:, 1, 0:NT], ssy[:, 0, 0:NT], 1.0 / SSM_W, EPS, ALU.mult, ALU.add)
            rsqrt_in(dve, nm_norm, ssy[:, 1, NT:3 * NT], ssy[:, 0, NT:3 * NT], ATT_W)
            rsqrt_out(dve, link, nm_norm, ssy[:, 2, :], ssy[:, 1, :], ssy[:, 3, :])
            dve.wait_ge(nm_norm.rstd, 1)
            tt(yn[:], yn[:], ssy[:, 2, 0:NT].unsqueeze(2).to_broadcast((P, TS, SSM_W)),
               ALU.mult).then_inc(y_scaled, 1)
            tt(ya_flat[:, :, 0:ATT_W], ya_flat[:, :, 0:ATT_W],
               ssy[:, 2, NT:2 * NT].unsqueeze(2).to_broadcast((P, NT, ATT_W)), ALU.mult).then_inc(y_scaled, 1)
            for n in range(2 * KT):
                k, h = n // 2, n % 2
                dve.wait_ge(mix_high, n + 1)
                dve.scalar_tensor_tensor(out=mix_view(op_lo, k, h), in0=mix_bank(k, n),
                                         scalar=g_sb[:, GAIN_MIX, k:k + 1], in1=mix_view(op_hi, k, h).bitcast(f32),
                                         op0=ALU.mult, op1=ALU.subtract).then_inc(mix_split, 1)

            def z_copy(c, m, j, n):
                ahead(split_low, dve, c, m, j)
                for h in range(2):
                    dve.wait_ge(mm_done, c * 2 + (h + 1))
                    dve.wait_ge(gains_in, 16)
                    dve.tensor_copy(z[:, n, half(h)], ps[:, 2 * j + h, :]).then_inc(evacuated, 1)

            steps(dve, C_OUT, C_OUT + KT, z_copy)

            def norm_out(norm, tmp):
                for h in range(2):
                    dve.wait_ge(norm.sums, h + 1)
                    rsqrt_in(dve, norm, tmp[:, 0, half(h)], ps[:, (4 if norm is nf_norm else 0) + h, :], D)
                for h in range(2):
                    rsqrt_out(dve, link, norm, rb[:, half(h)], tmp[:, 0, half(h)], tmp[:, 1, half(h)], h + 1)

            norm_out(no_norm, n2)
            order = [(h, k) for h in range(2) for k in range(KT)]
            for n in range(len(order) + 2):
                if n < len(order):
                    h, k = order[n]
                    dve.wait_ge(no_norm.rstd, h + 1)
                    tt(z[:, k, half(h)], z[:, k, half(h)], rb[:, half(h)], ALU.mult).then_inc(zn, 1)
                if 1 <= n <= len(order):
                    h, k = order[n - 1]
                    dve.wait_ge(zn, n)
                    dve.wait_ge(x_again[k], 16)
                    dve.scalar_tensor_tensor(out=x2[:, k, half(h)], in0=z[:, k, half(h)],
                                             scalar=g_sb[:, GAIN_POST, k:k + 1], in1=x2[:, k, half(h)],
                                             op0=ALU.mult, op1=ALU.add).then_inc(x2_done, 1)
                if n >= 2:
                    h, k = order[n - 2]
                    dve.wait_ge(h2_high, n - 1)
                    dve.scalar_tensor_tensor(out=op_lo[:, k, half(h)], in0=x2[:, k, half(h)],
                                             scalar=g_sb[:, GAIN_FFN_PRE, k:k + 1],
                                             in1=op_hi[:, k, half(h)].bitcast(f32), op0=ALU.mult,
                                             op1=ALU.subtract).then_inc(h2_split, 1)
            norm_out(nf_norm, n2)
            dve.wait_ge(nf_norm.rstd, 2)

            def gate_up(p_, gu):
                def step(c, m, j, n):
                    f = m - (gu // 2 - sum(PARTS[:p_]))
                    ahead(split_low, dve, c, m, j)
                    for h in range(2):
                        if j == 1:
                            if due(f * 2 + (h - 1)):
                                dve.wait_ge(hid_low, f * 2 + (h - 1))
                        dve.wait_ge(mm_done, c * 2 + (h + 1))
                        tt((tg if j == 0 else hf)[:, half(h)], ps[:, 2 * j + h, :], rb[:, half(h)],
                           ALU.mult).then_inc(evacuated, 1)
                    if j == 1:
                        for h in range(2):
                            dve.wait_ge(silu_done, f * 2 + (h + 1))
                            dve.wait_ge(evacuated, c * 2 + (h + 1))
                            tt(hf[:, half(h)], hf[:, half(h)], tg[:, half(h)], ALU.mult).then_inc(hf_done, 1)
                return step

            def down(p_, split=True):
                def step(c, m, j, n):
                    if split:
                        ahead(split_low, dve, c, m, j)
                    for h in range(2):
                        dve.wait_ge(mm_done, c * 2 + (h + 1))
                        dve.wait_ge(gains_in, 16)
                        if p_ == 0:
                            ins = dve.tensor_copy(z[:, n, half(h)], ps[:, 2 * j + h, :])
                        else:
                            ins = tt(z[:, n, half(h)], ps[:, 2 * j + h, :], z[:, n, half(h)], ALU.add)
                        ins.then_inc(evacuated, 1)
                return step

            for p_ in range(len(PARTS)):
                gu, dn = BASES[p_]
                steps(dve, gu, dn, gate_up(p_, gu), peel=2 if p_ == 0 else 0)
                if p_ < len(PARTS) - 1:
                    steps(dve, dn, dn + KT, down(p_))
                else:
                    steps(dve, dn, dn + KT - 2, down(p_))
                    down(p_)(dn + KT - 2, (dn + KT - 2) // 2, 0, KT - 2)
                    down(p_, False)(dn + KT - 1, (dn + KT - 2) // 2, 1, KT - 1)
            norm_out(ne_norm, r1["n3"])
            dve.wait_ge(x2_again, 16)
            for n in range(len(order) + 1):
                if n < len(order):
                    h, k = order[n]
                    dve.wait_ge(ne_norm.rstd, h + 1)
                    tt(z[:, k, half(h)], z[:, k, half(h)], rb[:, half(h)], ALU.mult).then_inc(ze, 1)
                if n >= 1:
                    h, k = order[n - 1]
                    dve.wait_ge(ze, n)
                    dve.scalar_tensor_tensor(out=z[:, k, half(h)], in0=z[:, k, half(h)],
                                             scalar=g_sb[:, GAIN_FFN_POST, k:k + 1], in1=r1["x2r"][:, k, half(h)],
                                             op0=ALU.mult, op1=ALU.add).then_inc(out_done, 1)

        @block.gpsimd
        def _(pool):
            chain = [0]

            def link(ins):
                chain[0] += 1
                ins.then_inc(pool_chain, 1)
                pool.wait_ge(pool_chain, chain[0])

            def tt(out, a, b, op):
                return pool.tensor_tensor(out, a, b, op)

            pool.memset(ident_b[:], 0.0)
            pool.memset(mask_b[:], 0.0)
            pool.memset(ident2[:], 0.0)
            link(pool.memset(ident[:], 0.0))
            for b in range(2):
                pool.affine_select(out=ident2[:], in_=ident2[:], compare_op=ALU.not_equal, fill=1.0, base=-DH * b,
                                   pattern=[[-1, DH]], channel_multiplier=1).then_inc(ident2_set, 1)
                pool.wait_ge(ident2_set, b + 1)
            for t in (ident, ident_b):
                pool.affine_select(out=t[:], in_=t[:], compare_op=ALU.not_equal, fill=1.0, base=0,
                                   pattern=[[-1, P]], channel_multiplier=1)
            pool.affine_select(out=mask_b[:], in_=mask_b[:], compare_op=ALU.is_ge, fill=MASKED, base=0,
                               pattern=[[P, QB], [-1, QB * P]], channel_multiplier=1).then_inc(ident_set, 1)
            pool.wait_ge(sq_x, 2)
            tt(acc1[:], sq1[:, 0, :], sq1[:, 1, :], ALU.add).then_inc(sq_added, 1)
            for k in range(2, KT):
                pool.wait_ge(sq_x, k + 1)
                pool.wait_ge(sq_added, k - 1)
                tt(acc1[:], acc1[:], sq1[:, k % 2, :], ALU.add).then_inc(sq_added, 1)

            pool.wait_ge(v_mm, NV * NT)
            pool.dma_start(wg[:], w_glu).then_inc(wg_in, 16)
            pool.dma_start(row[:], rows.partition_broadcast(P)).then_inc(row_in, 16)
            link(pool.memset(tz[:], 0.0))
            pool.wait_ge(powers, 1)
            shape = (P, NJ, TS + 1, CH)
            p_re, p_im = (pw[:, r].rearrange("p l j -> p j l") for r in range(2))
            t1, t2 = (pt[:, r].rearrange("p j (l o) -> p j l o", o=CH) for r in range(2))

            for l_ in range(TS + 1):
                pr_ = p_re[:, :, l_:l_ + 1].to_broadcast((P, NJ, CH))
                pi_ = p_im[:, :, l_:l_ + 1].to_broadcast((P, NJ, CH))
                tt(t1[:, :, l_], bc[:, 2], pr_, ALU.mult)
                tt(t2[:, :, l_], bc[:, 3], pi_, ALU.mult)
            link(pool.memset(ere[:, :, 0:1], 1.0))
            link(tt(dre[:].rearrange("p j l o -> p (j l o)"), pt[:, 0].rearrange("p j n -> p (j n)"),
                    pt[:, 1].rearrange("p j n -> p (j n)"), ALU.subtract))
            for l_ in range(TS + 1):
                pr_ = p_re[:, :, l_:l_ + 1].to_broadcast((P, NJ, CH))
                pi_ = p_im[:, :, l_:l_ + 1].to_broadcast((P, NJ, CH))
                tt(t1[:, :, l_], tb[:, 0], pi_, ALU.mult)
                tt(t2[:, :, l_], tb[:, 1], pr_, ALU.mult)
            link(pool.memset(eim[:, :, 0:1], 0.0))
            link(tt(dim_[:].rearrange("p j l o -> p (j l o)"), pt[:, 0].rearrange("p j n -> p (j n)"),
                    pt[:, 1].rearrange("p j n -> p (j n)"), ALU.add))
            pool.memset(pt[:, 0, 0:1, 0:1], 0.0).then_inc(d_done, 1)
            pool.wait_ge(d_done, 1)
            for b in range(7):
                n = 1 << b
                lo, hi = slice(0, n), slice(n, 2 * n)
                w_re, w_im = (wp[:, r, b, :].unsqueeze(2).to_broadcast((P, NJ, n)) for r in range(2))
                s1, s2 = (pt[:, r, :, 0:n] for r in range(2))
                s3, s4 = (pt[:, r, :, 64:64 + n] for r in range(2))
                tt(s1, ere[:, :, lo], w_re, ALU.mult)
                tt(s2, eim[:, :, lo], w_im, ALU.mult)
                tt(s3, ere[:, :, lo], w_im, ALU.mult)
                link(tt(s4, eim[:, :, lo], w_re, ALU.mult))
                tt(ere[:, :, hi], s1, s2, ALU.subtract)
                link(tt(eim[:, :, hi], s3, s4, ALU.add))
            pool.memset(pt[:, 0, 0:1, 0:1], 0.0).then_inc(e_done, 1)
            pool.wait_ge(row_in, 16)
            pool.wait_ge(ut_out, 1)
            for t in range(TS):
                ins = tt(ug[:, :, t, :], ug[:, :, t, :], row[:, 0, :].rearrange("p (g c) -> p g c", c=CH), ALU.mult)
            ins.then_inc(du_done, 1)
            pool.wait_ge(f_cum, 1)
            pool.dma_start(cum_dram, fz[:, 0, :]).then_inc(cum_out, 16)
            pool.wait_ge(kl_out, 1)
            for s in range(TS):
                pool.dma_start(tz[CH * s:CH * (s + 1), :, CH * s:P], kl[0:CH, :, 0:P - CH * s]).then_inc(tz_in, 16)

            def head_low(i, j):
                hc = i * 2 + j
                pool.wait_ge(qk_high_done, hc + 1)
                if due(hc):
                    pool.wait_ge(low_parts_done, i * 6 + 3 * j)
                tt(ql[0:DH, j, :], qq[0:DH, j, :], qa[0:DH, j, :].bitcast(f32), ALU.subtract).then_inc(low_parts_done, 1)
                pool.wait_ge(low_parts_done, i * 6 + (3 * j + 1))
                tt(ks[DH:P, j, :], kk[DH:P, j, :], ks[DH:P, j, :].bitcast(f32), ALU.subtract).then_inc(low_parts_done, 1)
                pool.wait_ge(low_parts_done, i * 6 + (3 * j + 2))
                pool.wait_ge(values_high_done, hc + 1)
                tt(vs[:, j, :, DH:P], vv[:, j, :, :], vs[:, j, :, 0:DH].bitcast(f32),
                   ALU.subtract).then_inc(low_parts_done, 1)

            for j in range(2):
                head_low(0, j)
            with pool.Fori(1, NH) as i:
                for j in range(2):
                    head_low(i, j)

            def add_squares(squares, acc, sq, n):
                for k in range(1, n):
                    pool.wait_ge(squares.sq, k + 1)
                    if k > 1:
                        pool.wait_ge(squares.added, k - 1)
                    a = sq(0) if k == 1 else acc
                    tt(acc, a, sq(k), ALU.add).then_inc(squares.added, 1)

            add_squares(zo_squares, acc2[:], lambda k: sq2[:, k % 2, :], KT)
            link(pool.memset(acc2b[:], 0.0))
            for h in range(2):
                for k in range(KT):
                    n = h * KT + k
                    pool.wait_ge(h2_squares.sq, n + 1)
                    if due(n):
                        pool.wait_ge(h2_squares.added, n)
                    tt(acc2b[:, half(h)], acc2b[:, half(h)], sq2b[:, n % 2, :], ALU.add).then_inc(h2_squares.added, 1)

            for p_, n in enumerate(PARTS):
                f0 = sum(PARTS[:p_])
                with pool.Fori(0, n) as i:
                    for h in range(2):
                        pool.wait_ge(hid_high, i * 2 + (2 * f0 + h + 1))
                        pool.wait_ge(x2_out, 16)
                        tt(hid_lo[:, i, half(h)], hf[:, half(h)], hid_hi[:, i, half(h)].bitcast(f32),
                           ALU.subtract).then_inc(hid_low, 1)
            add_squares(ff_squares, r1["acc3"][:], lambda k: r1["sq3"][:, k % 2, :], KT)

        @block.tensor
        def _(pe):
            for k in range(KT):
                pe.wait_ge(x_split, k + 1)
                pe.wait_ge(uf_split, k // 4 + 1)
                for s in range(TS):
                    out = ps[:, s, 0:UF]
                    pe.matmul(out, op_hi_c[:, k, s, :], ufh[:, k, :], start=k == 0, stop=False)
                    pe.matmul(out, op_hi_c[:, k, s, :], ufl[:, k, :], start=False, stop=False)
                    last = pe.matmul(out, op_lo_c[:, k, s, :], ufh[:, k, :], start=False, stop=k == KT - 1)
            last.then_inc(uf_mm, 1)
            pe.wait_ge(uf_copied, 1)
            pe.wait_ge(sq_added, KT - 1)
            pe.wait_ge(ones_set, 1)
            acc1_c = acc1[:].rearrange("p (c t) -> p t c", t=TS)
            for m in range(NT):
                pe.matmul(ps[:, 2, m:m + 1], acc1[:, m * P:(m + 1) * P], ones[:, 0:1], start=True, stop=True)
            for t in range(TS):
                last = pe.matmul(ps[:, 2, NT + t:NT + t + 1], acc1_c[:, t, :], ones[:, 0:1], start=True, stop=True)
            last.then_inc(n1s_norm.sums, 1)
            for h in range(2):
                norm_sums(pe, n1_norm, acc1, 0, h)
            for w in range(NV):
                pe.wait_ge(v_split, w + 1)
                for m in range(NT):
                    if due(NT * w + m - 3):
                        pe.wait_ge(v_scaled, NT * w + m - 3)
                    out = ps[:, 4 + m % 4, 0:VW]
                    tok = slice(m * P, (m + 1) * P)
                    for k in range(KT):
                        pe.matmul(out, op_hi[:, k, tok], vh[:, w % 2, k, :], start=k == 0, stop=False)
                        pe.matmul(out, op_hi[:, k, tok], vl[:, w % 2, k, :], start=False, stop=False)
                        last = pe.matmul(out, op_lo[:, k, tok], vh[:, w % 2, k, :], start=False, stop=k == KT - 1)
                    last.then_inc(v_mm, 1)
            pe.wait_ge(ident_set, 1)
            pe.wait_ge(uf_scaled, 1)
            pe.wait_ge(n1s_norm.mean, 1)
            for s in range(TS):
                last = pe.transpose(ps[0:NH, 2 + s // 4, (s % 4) * P:(s % 4 + 1) * P], fl[:, s, :], ident[:])
            last.then_inc(f_mm, 1)
            pe.wait_ge(v_scaled, NV * NT)
            for a in range(4):
                for b in range(4):
                    g = 4 * a + b
                    last = pe.transpose(ps[:, 4 + a, b * P:(b + 1) * P], ug[:, g, :, :].rearrange("p t c -> p (t c)"), ident[:])
                last.then_inc(ut_mm, 1)
            pe.wait_ge(n1_norm.mean, 1)
            pe.wait_ge(f_abs, 1)

            def qk_step(c, m, j, n):
                chunk_products(pe, c, j, op_hi, op_lo)

            steps(pe, 0, 4, qk_step, peel=4)
            pe.wait_ge(mt_done, 1)
            pe.wait_ge(ut_out, 1)
            for a in range(4):
                for b in range(4):
                    last = pe.transpose(ps[:, 4 + a, b * P:(b + 1) * P], mt[:, a // 2, 4 * (a % 2) + b, :], ident[:])
                last.then_inc(mb_mm, 1)
            pe.wait_ge(mb_out, 1)
            pe.wait_ge(d_done, 1)
            for a in range(4):
                for b in range(4):
                    g = group_at(a, b)
                    r, j = slice(ST * (g % 2), ST * (g % 2 + 1)), g // 2
                    out = ps[0:CH, 4 + a, b * P:(b + 1) * P]
                    pe.matmul(out, bbar[r, 0, j, :], dre[r, j, 0:TS, :], start=True, stop=False)
                    last = pe.matmul(out, bbar[r, 1, j, :], dim_[r, j, 0:TS, :], start=False, stop=True)
                last.then_inc(kl_mm, 1)
            pe.wait_ge(kl_out, 1)
            for r in range(2):
                for g in range(G):
                    j, rows_ = g // 2, slice(ST * (g % 2), ST * (g % 2 + 1))
                    last = pe.matmul(ps[rows_, 4 + 2 * r + j // 4, (j % 4) * NC:(j % 4 + 1) * NC],
                                     mb[:, r, j, rows_], ut[:, g, :], start=True, stop=True)
            last.then_inc(x_mm, 1)
            steps(pe, 4, 8, qk_step)
            pe.wait_ge(h_done, 1)
            pe.wait_ge(tz_in, 16 * TS)
            for g in range(G):
                j, r = g // 2, slice(ST * (g % 2), ST * (g % 2 + 1))
                a, b = bank_of(g)
                out = ps[:, 4 + a, b * P:(b + 1) * P]
                pe.matmul(out, ut[:, g, :], tz[:, g, :], start=True, stop=False)
                pe.matmul(out, hs[r, 0, j, :], dre[r, j, 1:TS + 1, :], start=False, stop=False)
                last = pe.matmul(out, hs[r, 1, j, :], dim_[r, j, 1:TS + 1, :], start=False, stop=True)
            last.then_inc(y_mm, 1)
            steps(pe, 8, 12, qk_step)
            pe.wait_ge(gelu_done, 1)
            for a in range(4):
                for b in range(4):
                    t, k = (4 * a + b) // 2, (4 * a + b) % 2
                    last = pe.transpose(ps[:, 4 + a, b * P:(b + 1) * P], yn[:, t, k * P:(k + 1) * P], ident[:])
                last.then_inc(gt_mm, 1)
            pe.wait_ge(gt_out, 1)
            pe.wait_ge(wg_in, 16)
            for t in range(TS):
                for k in range(2):
                    last = pe.matmul(ps[:, 4 + t // 2, (t % 2) * SSM_W:(t % 2 + 1) * SSM_W], gt[:, 2 * t + k, :],
                                     wg[:, k, :], start=k == 0, stop=k == 1)
            last.then_inc(glu_mm, 1)

            pe.wait_ge(glu_sum, 1)
            pe.wait_ge(evacuated, 2 * C_OUT)

            def scores(i, j, g, r):
                u, w = unit(i, j, g), (g + 1) * QB * P
                if g == ORDER[0] and r == 0:
                    pe.wait_ge(low_parts_done, i * 6 + (3 * j + 2))
                if due(u * 2 + (r - 1)):
                    pe.wait_ge(row_max_done, u * 2 + (r - 1))
                qs = slice((QB * g + r) * P, (QB * g + r + 1) * P)
                for b in range(-(-w // HALF)):
                    n = min(HALF, w - b * HALF)
                    out, key = ps[:, 2 * r + b, 0:n], slice(b * HALF, b * HALF + n)
                    masked = j == 1 and b == (w - 1) // HALF
                    pe.matmul(out, qa[:, j, qs], ks[:, j, key], start=True, stop=False)
                    last = pe.matmul(out, ql[0:DH, j, qs], ks[0:DH, j, key], start=False, stop=not masked)
                    if masked:
                        last = pe.matmul(ps[:, 2 * r + b, n - QB * P:n], ident_b[:], mask_b[:, r, :],
                                         start=False, stop=True)
                last.then_inc(qk_done, 1)

            def transposed(i, j, g, b):
                pc, slot = piece(i, j, g, b), slot_of(j, g, b)
                if b == 0:
                    pe.wait_ge(exp_done, unit(i, j, g) * 2 + 2)
                if due(pc - 1):
                    pe.wait_ge(pt_low_done, pc - 1)
                for a in range(2):
                    for r in range(QB):
                        last = pe.transpose(ps[:, 4 + slot % 2, (a * QB + r) * P:(a * QB + r + 1) * P],
                                            probs(g, r)[:, (2 * b + a) * P:(2 * b + a + 1) * P], ident[:])
                last.then_inc(pt_mm, 1)

            def outputs(i, j, g, b):
                slot = slot_of(j, g, b)
                if b == 0:
                    if due(unit(i, j, g) - 1):
                        pe.wait_ge(y_done, unit(i, j, g) - 1)
                    if g == ORDER[0]:
                        pe.wait_ge(low_parts_done, i * 6 + (3 * j + 3))
                pe.wait_ge(pt_low_done, piece(i, j, g, b) + 1)
                for a in range(2):
                    pe.matmul(outputs_bank(g), vs[:, j, 2 * b + a, :], pth[:, slot % 4, a, :],
                              start=b == 0 and a == 0, stop=False)
                    last = pe.matmul(outputs_bank(g), vs[:, j, 2 * b + a, :], ptl[:, slot % 4, a, :], start=False,
                                     stop=b == g and a == 1)
                last.then_inc(pv_done, 1)

            def y_back(i, j, g):
                pe.wait_ge(ot_done, unit(i, j, g) + 1)
                for r in range(QB):
                    last = pe.matmul(y_bank(g, r), ot[:, PLACE[g] % 2, r * P:(r + 1) * P], ident2[:], start=True, stop=True)
                last.then_inc(yt_mm, 1)

            def pe_unit(i, j, g, ahead_, prev, on, last):
                for b in range(max(g + 1, QB)):
                    if b < QB and ahead_:
                        scores(*ahead_, b)
                    if b <= g and on[b]:
                        transposed(*on[b])
                    if b <= g:
                        outputs(i, j, g, b)
                    if b == min(g, 1) and prev:
                        y_back(*prev)

            for g in ORDER[:2]:
                for r in range(QB):
                    scores(0, 0, g, r)
            for n in range(2):
                transposed(0, *PIECES[n])
            bodies(pe, pe_unit)
            y_back(NH - 1, *BODY[-1])

            pe.wait_ge(y_scaled, 2)
            pe.wait_ge(fox_scaled, 1)
            for n in range(2 * KT):
                k, h = n // 2, n % 2
                if due(n - 3):
                    pe.wait_ge(mix_split, n - 3)
                for a in range(4):
                    m = 4 * h + a
                    if k < SSM_W // P:
                        src = yn[:, m, k * P:(k + 1) * P]
                    else:
                        src = ya_flat[:, m, (k - 2) * P:(k - 1) * P]
                    last = pe.transpose(ps[:, 4 + n % 4, a * P:(a + 1) * P], src, ident[:])
                last.then_inc(mix_mm, 1)
            pe.wait_ge(mix_split, 2 * KT)

            def z_step(c, m, j, n):
                chunk_products(pe, c, j, op_hi, op_lo)

            steps(pe, C_OUT, C_OUT + KT, z_step)
            pe.wait_ge(zo_squares.added, KT - 1)
            for h in range(2):
                norm_sums(pe, no_norm, acc2, 0, h)
            pe.wait_ge(no_norm.mean, 2)
            chunk_products(pe, C_FFN, 0, op_hi, op_lo, before=lambda h, k: pe.wait_ge(h2_split, h * KT + k + 1))
            for h in range(2):
                pe.wait_ge(h2_squares.added, (h + 1) * KT)
                norm_sums(pe, nf_norm, acc2b, 4, h)
            chunk_products(pe, C_FFN + 1, 1, op_hi, op_lo)
            for p_, n in enumerate(PARTS):
                gu, dn = BASES[p_]
                steps(pe, gu + (2 if p_ == 0 else 0), dn, z_step)
                done = 2 * sum(PARTS[:p_ + 1])

                def down(c, m, j, n_, done=done, nk=PARTS[p_]):
                    def before(h, k):
                        if k == 0:
                            pe.wait_ge(hid_low, done - 2)
                        if k == nk - 1:
                            pe.wait_ge(hid_low, done - 1 + h)
                    chunk_products(pe, c, j, hid_hi, hid_lo, nk=nk, before=before)

                steps(pe, dn, dn + KT, down)
            pe.wait_ge(ff_squares.added, KT - 1)
            for h in range(2):
                norm_sums(pe, ne_norm, r1["acc3"], 0, h)
    return nc


def tiles(a):
    return np.ascontiguousarray(a.reshape(-1, P, a.shape[1]).transpose(1, 0, 2))


def chunks(a, width):
    r, c = a.shape
    return a.reshape(r // P, P, c // width, width).transpose(2, 1, 0, 3)


def layout(x, g_pre_mix, w_in, b_f, ssm_log_dt, ssm_a_re, ssm_a_im, ssm_b_re, ssm_b_im, ssm_c_re, ssm_c_im,
           ssm_d, w_glu, b_glu, g_mix, w_out, g_post_mix, g_pre_ffn, w_gate_up, w_down, g_post_ffn):
    w = w_in[0]
    o = SSM_W
    cols = {}
    for kind in ("dsa", "fox"):
        for part in "qkv":
            cols[kind + part] = w[:, o:o + ATT_W]
            o += ATT_W
    forget = w[:, o:o + NH]
    qk = [chunks(cols[n], P) for n in ("dsaq", "dsak", "foxq", "foxk")]
    gate, up = chunks(w_gate_up[0][:, :D_FF], P), chunks(w_gate_up[0][:, D_FF:], P)
    stream = [qk[n][p_] for p_ in range(NH // 2) for n in range(4)] + list(chunks(w_out[0], P))
    f = 0
    for p_, n in enumerate(PARTS):
        for t in range(f, f + n):
            stream += [gate[t], up[t]]
        down = list(chunks(w_down[0][f * P:(f + n) * P], P))
        f += n
        if p_ < len(PARTS) - 1:
            stream += down
    states = lambda a: a[0].reshape(NJ, 2 * ST).T
    by_state = lambda a: a[0].reshape(NJ, 2 * ST, CH).transpose(1, 0, 2)
    log_dt = np.repeat(ssm_log_dt[0][:, None], ST, axis=1)[None]
    lag = np.arange(P)[:, None] - (np.arange(LNC_W)[None, :] - (SEQ - P))
    count = sum(((lag >= 0) & (lag <= w_) & (lag % d == 0)).astype(np.int64) for w_, d in ((128, 1), (512, 4), (2048, 16)))
    lnc = np.where(count > 0, np.log(np.maximum(count, 1)), MASKED).astype(np.float32)
    return {
        "x_t": tiles(x[0].T),
        "gains": np.stack([g[0].reshape(KT, P).T for g in (g_pre_mix, g_mix, g_post_mix, g_pre_ffn, g_post_ffn)], 1),
        "w_uf": tiles(np.concatenate([w[:, :SSM_W], forget], axis=1)),
        "w_v": chunks(np.concatenate([cols["dsav"], cols["foxv"]], axis=1), VW),
        "w_stream": np.stack(stream),
        "w_last": np.stack(down),
        "s_par": np.stack([states(log_dt), states(ssm_a_re), states(ssm_a_im)], 1),
        "s_bc": np.stack([by_state(ssm_b_re), by_state(ssm_b_im), by_state(ssm_c_re.transpose(0, 1, 3, 2)),
                          by_state(ssm_c_im.transpose(0, 1, 3, 2))], 1),
        "rows": np.stack([ssm_d[0], b_glu[0]]),
        "w_glu": tiles(w_glu[0]),
        "b_f": b_f[0][:, None],
        "lnc_dram": lnc,
    }


def kernel(**inputs):
    import concourse.bacc as bacc
    from concourse.bass_utils import run_bass_kernel_spmd

    nc = bacc.Bacc("TRN2", target_bir_lowering=False, num_devices=1)
    arrays = {n: np.ascontiguousarray(a) for n, a in layout(**{n: np.asarray(a) for n, a in inputs.items()}).items()}
    args = {n: nc.dram_tensor(n, a.shape, mybir.dt.from_np(a.dtype), kind="ExternalInput").ap()
            for n, a in arrays.items()}
    out = nc.dram_tensor("out_t", (P, KT, SEQ), mybir.dt.float32, kind="ExternalOutput").ap()
    block_kernel(nc, out_t=out, **args)
    got = run_bass_kernel_spmd(nc, [arrays], core_ids=[0]).results[0]["out_t"]
    return np.ascontiguousarray(got.transpose(1, 0, 2).reshape(D, SEQ).T)[None]
```

```python
import math
from contextlib import ExitStack

import numpy as np

import concourse.bass as bass
from concourse import mybir

P = 128
D = 1024
SEQ = 1024
KT = D // P
NT = SEQ // P
HALF = 512
DH = 64
NH = 6
SSM_W = 256
G, CH, ST = 16, 16, 64
TS = 8
NC = SEQ // TS
NJ = G // 2
ATT_W = NH * DH
D_FF = 2816
FT = D_FF // P
PARTS = (8, 8, 6)
UF = SSM_W + NH
VW = 256
NV = 2 * ATT_W // VW
EPS = 1e-6
MASKED = -1e30
QB = 2
UNITS = NT // QB
ORDER = (3, 0, 2, 1)
PLACE = tuple(ORDER.index(g) for g in range(UNITS))
LNC_W = SEQ - P + QB * P
PCS = UNITS * (UNITS + 1) // 2
PR_W = QB * QB * P * PCS

C_QK = 0
C_OUT = C_QK + 4 * NH // 2
C_OUT2 = C_OUT + KT
C_FFN = C_OUT2 + KT


class NormSemaphores:

    def __init__(self, sem, name):
        self.sums = sem(name + "_sums")
        self.mean = sem(name + "_mean")
        self.seed = sem(name + "_seed")
        self.rstd = sem(name + "_rstd")


class SquareSemaphores:

    def __init__(self, sem, name):
        self.sq = sem(name + "_sq")
        self.added = sem(name + "_added")


def block_kernel(nc, x_t, gains, w_uf, w_v, w_stream, w_last, s_par, s_bc, rows, w_glu, b_f,
                 lnc_dram, out_t):
    f32, f32r, bf16 = mybir.dt.float32, mybir.dt.float32r, mybir.dt.bfloat16
    ALU, ACT, AX = mybir.AluOpType, mybir.ActivationFunctionType, mybir.AxisListType

    ctx = ExitStack()
    with ctx:
        qk_dram = nc.dram_tensor("qk_scratch", (2, 4, NH // 2, P, SEQ), f32, kind="Internal").ap()
        v_dram = nc.dram_tensor("v_scratch", (2 * NH, P, NT, DH), f32, kind="Internal").ap()
        cum_dram = nc.dram_tensor("cum_scratch", (NH, SEQ), f32, kind="Internal").ap()
        x2_dram = nc.dram_tensor("x2_scratch", (P, KT, SEQ), f32, kind="Internal").ap()
        qk_heads = qk_dram.rearrange("x a c (b d) n -> x a (c b) d n", b=2)

        def sem(name):
            return ctx.enter_context(nc.semaphore(name))

        def sem_list(name, n):
            return [sem(f"{name}{i}") for i in range(n)]

        par_in, bc_in, gains_in, bf_in, wg_in, row_in, lnc_in = (sem(n) for n in (
            "par_in", "bc_in", "gains_in", "bf_in", "wg_in", "row_in", "lnc_in"))
        ln_done = sem("ln_done")
        x_in, uf_in = sem_list("x_in", KT), sem_list("uf_in", KT // 2)
        ones_set, ident_set, ident2_set = sem("ones_set"), sem("ident_set"), sem("ident2_set")
        dve_chain, pool_chain, dve_waited = sem("dve_chain"), sem("pool_chain"), sem("dve_waited")
        w_loaded = sem_list("w_loaded", 2)
        w_high, w_split, mm_done, evacuated = (sem(n) for n in ("w_high", "w_split", "mm_done", "evacuated"))
        x_high, x_split, sq_x, sq_added, uf_high, uf_split, uf_mm, uf_copied, uf_scaled = (sem(n) for n in (
            "x_high", "x_split", "sq_x", "sq_added", "uf_high", "uf_split", "uf_mm", "uf_copied", "uf_scaled"))
        v_in, v_high_done, v_split, v_mm, v_scaled, v_out = (sem(n) for n in (
            "v_in", "v_high_done", "v_split", "v_mm", "v_scaled", "v_out"))
        f_mm, f_abs, f_exp, f_ln, f_cum, cum_out = (sem(n) for n in (
            "f_mm", "f_abs", "f_exp", "f_ln", "f_cum", "cum_out"))
        qk_high, qk_low, qk_out = sem("qk_high"), sem("qk_low"), sem_list("qk_out", 2)
        par_act, par_dve, powers, ut_mm, ut_out, mt_done, mb_mm, mb_out = (sem(n) for n in (
            "par_act", "par_dve", "powers", "ut_mm", "ut_out", "mt_done", "mb_mm", "mb_out"))
        d_done, e_done, kl_mm, kl_out, tz_zero, tz_in, x_mm, h_done, du_done, y_mm, y_sum = (sem(n) for n in (
            "d_done", "e_done", "kl_mm", "kl_out", "tz_zero", "tz_in", "x_mm", "h_done", "du_done", "y_mm", "y_sum"))
        gelu_done, gt_mm, gt_out, glu_mm, glu_sum, glu_sig, y_gated, y_ssm_sq = (sem(n) for n in (
            "gelu_done", "gt_mm", "gt_out", "glu_mm", "glu_sum", "glu_sig", "y_gated", "y_ssm_sq"))
        staged, values_in, fb_in = sem_list("staged", 2), sem_list("values_in", 2), sem("fb_in")
        values_high_done, values_low_done, qk_done, row_max_done, exp_done, pt_mm, pt_high_done, pt_low_done = (
            sem(n) for n in ("values_high_done", "values_low_done", "qk_done", "row_max_done", "exp_done", "pt_mm",
                             "pt_high_done", "pt_low_done"))
        pv_done, ot_done, yt_mm, rden_done, y_done = (sem(n) for n in (
            "pv_done", "ot_done", "yt_mm", "rden_done", "y_done"))
        y_att_sq, y_scaled, fox_scaled, mix_mm, mix_high, mix_split = (sem(n) for n in (
            "y_att_sq", "y_scaled", "fox_scaled", "mix_mm", "mix_high", "mix_split"))
        zn, x2_done, h2_high, h2_split, x2_out, x2_again = (sem(n) for n in (
            "zn", "x2_done", "h2_high", "h2_split", "x2_out", "x2_again"))
        silu_done, hf_done, hid_high, hid_low = (sem(n) for n in ("silu_done", "hf_done", "hid_high", "hid_low"))
        ze, out_done, out_done_pool, z_gained, out_stored = (sem(n) for n in (
            "ze", "out_done", "out_done_pool", "z_gained", "out_stored"))
        n1s_norm, n1_norm, nm_norm, no_norm, nf_norm, ne_norm = (NormSemaphores(sem, n) for n in (
            "n1s", "n1", "nm", "no", "nf", "ne"))
        zo_squares, h2_squares, ff_squares = (SquareSemaphores(sem, n) for n in ("zo", "h2", "ff"))

        def due(count):
            return not isinstance(count, int) or count > 0

        def sb(name, shape, dt=f32):
            return ctx.enter_context(nc.sbuf_tensor(name, shape, dt))

        def region(name, nbytes, *phases):
            out = {}
            for tensors in phases:
                with ExitStack() as phase:
                    for n, shape, dt in tensors:
                        out[n] = phase.enter_context(nc.sbuf_tensor(n, shape, dt))
            ctx.enter_context(nc.sbuf_tensor(name, [P, nbytes], mybir.dt.uint8))
            return out

        KB = 1024
        r1 = region("operand_region", 64 * KB,
                    [("op_hi", [P, KT, SEQ], f32r), ("op_lo", [P, KT, SEQ], f32r)],
                    [("sc", [P, QB, SEQ], f32), ("pr", [P, PR_W], f32), ("fb", [P, SEQ], f32),
                     ("ot", [P, 2, QB * P], f32), ("y_sq", [P, 2, NT, DH], f32),
                     ("y_sq_sum", [P, 2, NT, DH], f32)],
                    [("x2r", [P, KT, SEQ], f32), ("sq3", [P, 2, SEQ], f32), ("acc3", [P, SEQ], f32),
                     ("n3", [P, 2, SEQ], f32)])
        op_hi, op_lo = r1["op_hi"], r1["op_lo"]
        sc, pr, fb, ot, y_sq, y_sq_sum = (r1[n] for n in ("sc", "pr", "fb", "ot", "y_sq", "y_sq_sum"))
        r2 = region("hidden_region", 64 * KB,
                    [("ufh", [P, KT, UF], f32r), ("ufl", [P, KT, UF], f32r), ("uf_raw", [P, KT, UF], f32),
                     ("acc1", [P, SEQ], f32), ("vh", [P, 2, KT, VW], f32r), ("vl", [P, 2, KT, VW], f32r)],
                    [("dre", [P, NJ, TS + 1, CH], f32), ("dim", [P, NJ, TS + 1, CH], f32),
                     ("ere", [P, NJ, NC], f32), ("eim", [P, NJ, NC], f32), ("pt", [P, 2, NJ, (TS + 1) * CH], f32),
                     ("ut", [P, G, NC], f32),
                     ("tz", [P, G, P], f32), ("mt", [P, 2, NJ, P], f32), ("mb", [P, 2, NJ, P], f32),
                     ("wg", [P, 2, SSM_W], f32), ("row", [P, 2, SSM_W], f32)],
                    [("qa", [P, 2, SEQ], f32r), ("ql", [P, 2, SEQ], f32r), ("ks", [P, 2, SEQ], f32r),
                     ("vs", [P, 2, NT, P], f32r), ("pth", [P, 4, 2, QB * P], f32r),
                     ("ptl", [P, 4, 2, QB * P], f32r), ("vv", [P, 2, NT, DH], f32), ("lnc", [P, LNC_W], f32)],
                    [("x2", [P, KT, SEQ], f32), ("sq2", [P, 2, SEQ], f32), ("acc2", [P, SEQ], f32),
                     ("acc2b", [P, SEQ], f32), ("n2", [P, 2, SEQ], f32), ("sq2b", [P, 2, HALF], f32),
                     ("nf_rstd", [P, HALF], f32)],
                    [("hid_hi", [P, 8, SEQ], f32r), ("hid_lo", [P, 8, SEQ], f32r)])
        ufh, ufl, vh, vl, uf_raw, acc1 = (r2[n] for n in ("ufh", "ufl", "vh", "vl", "uf_raw", "acc1"))
        dre, dim_, ere, eim, ut, tz, mt, mb, pt, wg, row = (r2[n] for n in
            ("dre", "dim", "ere", "eim", "ut", "tz", "mt", "mb", "pt", "wg", "row"))
        qa, ql, ks, vs, pth, ptl, vv, lnc = (r2[n] for n in ("qa", "ql", "ks", "vs", "pth", "ptl", "vv", "lnc"))
        x2, sq2, acc2, acc2b, n2, sq2b, nf_rstd = (r2[n] for n in (
            "x2", "sq2", "acc2", "acc2b", "n2", "sq2b", "nf_rstd"))
        hid_hi, hid_lo = r2["hid_hi"], r2["hid_lo"]
        r3 = region("sum_region", 32 * KB,
                    [("xt", [P, KT, SEQ], f32)],
                    [("vst", [P, NV, NT, VW], f32)],
                    [("hs", [P, 2, NJ, NC], f32), ("qk_hi", [P, 2, SEQ], f32r), ("qko", [P, 2, SEQ], f32),
                     ("yn", [P, TS, SSM_W], f32)],
                    [("skip_lo", [P, 16 * KB], mybir.dt.uint8), ("qk_lo", [P, 2, SEQ], f32r)],
                    [("skip_fz", [P, 24 * KB], mybir.dt.uint8), ("fz", [NH, 2, SEQ], f32)],
                    [("ya", [P, NT, 2 * NH, DH], f32)],
                    [("z", [P, KT, SEQ], f32)])
        xt, vst, hs, qk_hi, qk_lo, qko, yn, fz, ya, z = (r3[n] for n in
            ("xt", "vst", "hs", "qk_hi", "qk_lo", "qko", "yn", "fz", "ya", "z"))
        r4 = region("chunk_region", 16 * KB,
                    [("w_hi", [P, 2, KT, P], f32r), ("w_lo", [P, 2, KT, P], f32r)],
                    [("sq1", [P, 2, SEQ], f32), ("n1", [P, 2, SEQ], f32)])
        w_hi, w_lo, sq1, n1 = (r4[n] for n in ("w_hi", "w_lo", "sq1", "n1"))
        w_raw = sb("w_raw", [P, 2, KT, P])
        r5 = region("small_region", 4 * TS * UF + 64,
                    [("ug", [P, G, TS, CH], f32), ("fl", [P, TS, NH], f32)],
                    [("tg", [P, SEQ], f32), ("hf", [P, SEQ], f32)])
        ug, fl, tg, hf = r5["ug"], r5["fl"], r5["tg"], r5["hf"]
        rb = sb("rb", [P, SEQ])
        g_sb = sb("g_sb", [P, 5, KT])
        ident = sb("ident", [P, P])
        ident2 = sb("ident2", [P, DH])
        ident_b = sb("ident_b", [P, P], bf16)
        mask_b = sb("mask_b", [P, QB, QB * P], bf16)
        ones = sb("ones", [P, P])
        sp = sb("sp", [P, 24, NJ])
        bc = sb("bc", [P, 4, NJ, CH])
        bbar = sb("bbar", [P, 2, NJ, CH])
        tb = sb("tb", [P, 2, NJ, CH])
        pw = sb("pw", [P, 2, TS + 1, NJ])
        pw_back = sb("pw_back", [P, 2, TS, NJ])
        warm = sb("warm", [P, 16])
        rn = sb("rn", [P, 4, 2 * NT])
        nm = sb("nm", [P, UNITS, QB])
        den = sb("den", [P, UNITS, QB])
        rden = sb("rden", [P, 2, QB])
        wp = sb("wp", [P, 2, 8, NJ])
        ssy = sb("ssy", [P, 4, 3 * NT])
        bfs = sb("bfs", [NH, 1])

        ps = ctx.enter_context(nc.psum_tensor("ps", [P, 8, HALF], f32))

        (LDT, AR, AI, DT, ARDT, TH, DEC, RHO, KR, RR, SN, SH, CS, ABR, ABI, M1, MAG, CR, CI, TA, TB_, T1, T2,
         TC) = range(24)

        def q(n):
            return sp[:, n, :]

        GAIN_PRE, GAIN_MIX, GAIN_POST, GAIN_FFN_PRE, GAIN_FFN_POST = range(5)

        OUT_TILES = ((), (), (0,), (1,), (2,), (3,), (4,), (5,))
        OUT_DVE = 5

        ss = mb
        op_hi_c = op_hi[:].rearrange("p k (c t) -> p k t c", t=TS)
        op_lo_c = op_lo[:].rearrange("p k (c t) -> p k t c", t=TS)
        kl = hs[:].rearrange("p r j c -> p (r j) c")
        gt = mt[:].rearrange("p r j c -> p (r j) c")
        sg = mb[:].rearrange("p r j c -> p (r j c)").rearrange("p (t n) -> p t n", t=TS)
        ya_flat = ya[:].rearrange("p m h d -> p m (h d)")
        ssy_flat = ssy[:].rearrange("p a n -> p (a n)")
        v_raw = w_raw[:].rearrange("p s k n -> p (s k n)").rearrange("p (k n) -> p k n", n=VW)

        def half(h):
            return slice(h * HALF, (h + 1) * HALF)

        def mix_view(op, k, h):
            if k < SSM_W // P:
                return (op_hi_c if op is op_hi else op_lo_c)[:, k, 4 * h:4 * h + 4, :]
            return op[:, k, half(h)]

        MIX = ([(k, h) for k in range(SSM_W // P) for h in range(2)]
               + [(k, h) for h in range(2) for k in range(SSM_W // P, KT)])
        MIX_FIRST = len(MIX) - (KT - SSM_W // P)

        def mix_bank(k, n):
            bank = ps[:, 4 + n % 4, :]
            return bank.rearrange("p (t c) -> p t c", t=4) if k < SSM_W // P else bank

        block = ctx.enter_context(nc.Block())

        def ffn_bases():
            c, out = C_FFN, []
            for n in PARTS:
                out.append((c, c + 2 * n))
                c += 2 * n + KT
            return out, c

        BASES, C_DOWN2 = ffn_bases()
        C_END = C_DOWN2 + KT

        def steps(e, lo, hi, step, peel=0):
            for c in range(lo, lo + peel):
                step(c, c // 2, c % 2, c - lo)
            if hi > lo + peel:
                with e.Fori(0, (hi - lo - peel) // 2) as i:
                    for j in range(2):
                        step(i * 2 + (lo + peel + j), i + (lo + peel) // 2, j, i * 2 + (peel + j))

        def load_chunk(e, c, m, j, src, nk=KT):
            if due(c - 1):
                e.wait_ge(w_split, c - 1)
            e.dma_start(w_raw[:, j, 0:nk, :], src).then_inc(w_loaded[j], 16)

        def split_high(e, c, m, j):
            if due(c * 2 - 2):
                e.wait_ge(mm_done, c * 2 - 2)
            e.wait_ge(w_loaded[j], m * 16 + 16)
            e.activation(w_hi[:, j, :, :], w_raw[:, j, :, :], ACT.Copy).then_inc(w_high, 1)

        def split_low(e, c, m, j):
            e.wait_ge(w_high, c + 1)
            e.tensor_tensor(w_lo[:, j, :, :], w_raw[:, j, :, :], w_hi[:, j, :, :].bitcast(f32),
                            ALU.subtract).then_inc(w_split, 1)

        def ahead(split, e, c, m, j):
            split(e, c + 1, m + j, 1 - j)

        def chunk_products(e, c, j, x_hi, x_lo, nk=KT, before=None, late=0):
            e.wait_ge(w_split, c + 1)
            for h in range(2):
                if due(c * 2 + (h - 3) + h * late):
                    e.wait_ge(evacuated, c * 2 + (h - 3) + h * late)
                out = ps[:, 2 * j + h, :]
                for k in range(nk):
                    if before:
                        before(h, k)
                    e.matmul(out, w_hi[:, j, k, :], x_hi[:, k, half(h)], start=k == 0, stop=False)
                    e.matmul(out, w_hi[:, j, k, :], x_lo[:, k, half(h)], start=False, stop=False)
                    last = e.matmul(out, w_lo[:, j, k, :], x_hi[:, k, half(h)], start=False, stop=k == nk - 1)
                last.then_inc(mm_done, 1)

        def half_products(e, c, j, h, x_hi, x_lo, nk=KT, before=None):
            e.wait_ge(w_split, c + 1)
            e.wait_ge(evacuated, c * 2 - 2)
            out = ps[:, 2 * j, :]
            for k in range(nk):
                if before:
                    before(k)
                e.matmul(out, w_hi[:, j, k, :], x_hi[:, k, half(h)], start=k == 0, stop=False)
                e.matmul(out, w_hi[:, j, k, :], x_lo[:, k, half(h)], start=False, stop=False)
                last = e.matmul(out, w_lo[:, j, k, :], x_hi[:, k, half(h)], start=False, stop=k == nk - 1)
            last.then_inc(mm_done, 2)

        def norm_sums(e, norm, acc, bank, h):
            e.matmul(ps[:, bank + h, :], ones[:], acc[:, half(h)], start=True,
                     stop=True).then_inc(norm.sums, 1)

        logs = [0]

        def rsqrt_in(e, norm, v, sums, n):
            e.tensor_scalar(v, sums, 1.0 / n, EPS, ALU.mult, ALU.add).then_inc(norm.mean, 1)

        def rsqrt_act(e, norm, y, v, count=1):
            e.activation(warm[:, logs[0]:logs[0] + 1], ones[:, 0:1], ACT.Ln)
            e.wait_ge(norm.mean, count)
            logs[0] += 1
            e.activation(y, v, ACT.Ln).then_inc(ln_done, 1)
            e.wait_ge(ln_done, logs[0])
            e.activation(y, y, ACT.Exp, scale=-0.5).then_inc(norm.seed, 1)

        def rsqrt_out(e, link, norm, y, v, t, count=1):
            e.wait_ge(norm.seed, count)
            link(e.tensor_tensor(t, y, y, ALU.mult))
            link(e.tensor_tensor(t, t, v, ALU.mult))
            link(e.tensor_scalar(t, t, -0.5, 1.5, ALU.mult, ALU.add))
            e.tensor_tensor(y, y, t, ALU.mult).then_inc(norm.rstd, 1)

        @block.sync
        def _(sync):
            sync.dma_start(g_sb[:], gains).then_inc(gains_in, 16)
            sync.dma_start(sp[:, 0:3, :], s_par).then_inc(par_in, 16)
            for k in range(KT):
                sync.dma_start(xt[:, k, :], x_t[:, k, :]).then_inc(x_in[k], 16)
                if k % 2 == 0:
                    sync.dma_start(uf_raw[:, k:k + 2, :], w_uf[:, k:k + 2, :]).then_inc(uf_in[k // 2], 16)
            sync.dma_start(bc[:], s_bc).then_inc(bc_in, 16)
            sync.dma_start(bfs[:], b_f).then_inc(bf_in, 16)
            for w in range(NV):
                if due(w):
                    sync.wait_ge(v_split, w)
                sync.dma_start(v_raw, w_v[w]).then_inc(v_in, 16)
            sync.wait_ge(v_split, NV)
            for j in range(2):
                load_chunk(sync, j, 0, j, w_stream[j])
            for w in range(NV):
                sync.wait_ge(v_scaled, NT * (w + 1))
                for h in range(4):
                    sync.dma_start(v_dram[4 * w + h], vst[:, w, :, h * DH:(h + 1) * DH]).then_inc(v_out, 16)

            def qk_load(c, j):
                sync.wait_ge(w_split, c + 1)
                sync.dma_start(w_raw[:, j, :, :], w_stream[c + 2]).then_inc(w_loaded[j], 16)

            def qk_store(c, j, kind, part):
                sync.wait_ge(qk_high, c + 1)
                sync.dma_start(qk_dram[0, kind, part], qk_hi[:, j, :].bitcast(f32)).then_inc(qk_out[j], 16)
                sync.wait_ge(qk_low, c + 1)
                sync.dma_start(qk_dram[1, kind, part], qk_lo[:, j, :].bitcast(f32)).then_inc(qk_out[j], 16)

            for part in range(NH // 2 - 1):
                with sync.Fori(0, 2) as i:
                    for j in range(2):
                        qk_load(i * 2 + (4 * part + j), j)
                        qk_store(i * 2 + (4 * part + j), j, i * 2 + j, part)

            def stage_values(i, j, hc):
                if due(hc - 1):
                    sync.wait_ge(values_low_done, hc - 1)
                sync.dma_start(vv[:, j, :, :], v_dram[i + NH * j]).then_inc(values_in[j], 16)

            def stage_bias(i, hc):
                if due(hc * NT - NT):
                    sync.wait_ge(row_max_done, hc * NT - NT)
                sync.dma_start(fb[:], cum_dram[i].partition_broadcast(P)).then_inc(fb_in, 16)

            for c in range(4 * (NH // 2 - 1), C_OUT):
                qk_load(c, c % 2)
                if c == C_OUT - 1:
                    sync.wait_ge(v_out, 16 * 4 * NV)
                    sync.wait_ge(y_ssm_sq, 1)
                    stage_values(0, 0, 0)
                    sync.dma_start(lnc[:], lnc_dram).then_inc(lnc_in, 16)
                    stage_values(0, 1, 1)
                qk_store(c, c % 2, c % 4, c // 4)
            sync.wait_ge(mm_done, 2 * C_OUT)
            sync.wait_ge(cum_out, 16)
            stage_bias(0, 1)
            with sync.Fori(1, NH) as i:
                stage_values(i, 0, i * 2)
                stage_values(i, 1, i * 2 + 1)
                stage_bias(i, i * 2 + 1)

            sync.wait_ge(pv_done, 2 * NH * 10)
            for k in range(KT):
                sync.dma_start(x2[:, k, :], x_t[:, k, :]).then_inc(x_in[k], 16)
            with sync.Fori(0, KT // 2 - 1) as i:
                for j in range(2):
                    c = i * 2 + (C_OUT + 2 + j)
                    load_chunk(sync, c, i + (C_OUT + 2) // 2, j, w_stream[c])
            last = BASES[-1][1]
            for first, end in ((C_OUT2, C_FFN + 2), (C_FFN + 2, C_FFN + 4), (C_FFN + 4, last)):
                with sync.Fori(0, (end - first) // 2) as i:
                    for j in range(2):
                        load_chunk(sync, i * 2 + (first + j), i + first // 2, j, w_stream[i * 2 + (first + j - KT)])
                if end < last:
                    h = 0 if first == C_OUT2 else 1
                    sync.wait_ge(x2_done, (h + 1) * KT)
                    sync.dma_start(x2_dram[:, :, half(h)], x2[:, :, half(h)]).then_inc(x2_out, 16)
            for c in range(2 * KT):
                load_chunk(sync, last + c, (last + c) // 2, c % 2, w_last[c % KT], PARTS[-1])
                if 1 <= c <= KT:
                    sync.wait_ge(x2_out, 16 * 2)
                    sync.wait_ge(mm_done, 2 * last)
                    sync.dma_start(r1["x2r"][:, c - 1, :], x2_dram[:, c - 1, :]).then_inc(x2_again, 16)
            for h in range(2):
                for k in range(KT):
                    if h == 1 and k >= OUT_DVE:
                        sync.wait_ge(out_done_pool, k + 1 - OUT_DVE)
                    else:
                        sync.wait_ge(out_done, h * KT + k + 1)
                    sync.dma_start(out_t[:, k, half(h)], z[:, k, half(h)]).then_inc(out_stored, 16)
            sync.wait_ge(out_stored, 16 * 2 * KT)

        def quarter(a):
            return ps[:, 4 + a, :].rearrange("p (g c) -> p g c", g=4)

        def group_at(a, b):
            return 2 * (4 * (a % 2) + b) + a // 2

        def bank_of(g):
            return 2 * (g % 2) + g // 8, g // 2 % 4

        BODY = [(j, g) for j in range(2) for g in ORDER]
        PIECES = [(j, g, b) for j, g in BODY for b in range(g + 1)]

        def piece(i, j, g, b):
            return i * (2 * PCS) + slot_of(j, g, b)

        def slot_of(j, g, b):
            return j * PCS + sum(f + 1 for f in ORDER[:PLACE[g]]) + b

        def unit(i, j, g):
            return i * (2 * UNITS) + (j * UNITS + PLACE[g])

        def shifted(seq, i, n, by, last):
            n += by
            if n >= len(seq):
                return None if last else (i + 1, *seq[n - len(seq)])
            return (i, *seq[n])

        def bodies(e, step):
            def body(i, first, last):
                for n, (j, g) in enumerate(BODY):
                    prev = (i, *BODY[n - 1]) if n else (None if first else (i - 1, *BODY[-1]))
                    on = [shifted(PIECES, i, slot_of(j, g, b), 2, last) for b in range(g + 1)]
                    step(i, j, g, shifted(BODY, i, n, 2, last), prev, on, last)
            body(0, True, False)
            with e.Fori(1, NH - 1) as i:
                body(i, False, False)
            body(NH - 1, False, True)

        def probs(g, r):
            w = (g + 1) * QB * P
            at = QB * QB * P * g * (g + 1) // 2 + r * w
            return pr[:, at:at + w]

        def outputs_bank(g):
            return ps[:, 6 + PLACE[g] % 2, 0:QB * P]

        def y_bank(g, r):
            return ps[:, 6 + PLACE[g] % 2, QB * P + r * DH:QB * P + (r + 1) * DH]

        @block.scalar
        def _(act):
            act.wait_ge(ones_set, 1)
            act.activation(warm[:, 15:16], ones[:, 0:1], ACT.Copy)
            act.wait_ge(gains_in, 16)
            for k in range(KT):
                act.wait_ge(x_in[k], 16)
                act.activation(op_hi[:, k, :], xt[:, k, :], ACT.Copy,
                               scale=g_sb[:, GAIN_PRE, k:k + 1]).then_inc(x_high, 1)
                if k % 2 == 0:
                    act.wait_ge(uf_in[k // 2], 16)
                    act.activation(ufh[:, k:k + 2, :], uf_raw[:, k:k + 2, :], ACT.Copy).then_inc(uf_high, 1)
                if k >= 2:
                    act.wait_ge(sq_added, max(1, k - 2))
                act.activation(sq1[:, k % 2, :], xt[:, k, :], ACT.Square).then_inc(sq_x, 1)
                if k == 1:
                    act.wait_ge(par_in, 16)
                    act.activation(q(DT), q(LDT), ACT.Exp).then_inc(par_act, 1)
                if k == 2:
                    act.wait_ge(par_dve, 1)
                    act.activation(q(DEC), q(ARDT), ACT.Exp)
                    act.activation(q(RHO), q(ARDT), ACT.Exp, scale=float(TS)).then_inc(par_act, 1)
                if k == 4:
                    act.wait_ge(par_dve, 2)
                    act.activation(q(SN), q(RR), ACT.Sin)
                    act.activation(q(SH), q(RR), ACT.Sin, scale=0.5).then_inc(par_act, 1)

            def v_high(w):
                act.wait_ge(v_in, 16 * (w + 1))
                if due(NT * (w - 1)):
                    act.wait_ge(v_mm, NT * (w - 1))
                act.activation(vh[:, w % 2, :, :], v_raw, ACT.Copy).then_inc(v_high_done, 1)

            v_high(0)
            act.wait_ge(uf_mm, 1)
            act.activation(fl[:], ps[:, :, SSM_W:UF], ACT.Copy).then_inc(uf_copied, 1)
            for s in (4, 5, 6, 7, 0, 1, 2, 3):
                act.activation(ug[:, :, s, :], ps[:, s, 0:SSM_W].rearrange("p (g c) -> p g c", c=CH),
                               ACT.Copy).then_inc(uf_copied, 1)
            rsqrt_act(act, n1s_norm, rn[:, 0, :], rn[:, 1, :])
            act.wait_ge(n1s_norm.rstd, 1)
            act.wait_ge(x_split, KT)
            for w in range(NV):
                if w + 1 < NV:
                    v_high(w + 1)
                for m in range(NT):
                    if w == 0 and m == 4:
                        rsqrt_act(act, n1_norm, rb[:], n1[:, 0, :])
                    if w == NV - 1 and m == 4:
                        act.wait_ge(n1_norm.rstd, 1)
                        split_high(act, 0, 0, 0)
                    act.wait_ge(v_mm, NT * w + m + 1)
                    act.activation(vst[:, w, m, :], ps[:, 4 + m % 4, 0:VW], ACT.Copy,
                                   scale=rn[:, 0, m:m + 1]).then_inc(v_scaled, 1)
            act.wait_ge(f_abs, 1)
            act.activation(fz[:, 1, :], fz[:, 1, :], ACT.Exp).then_inc(f_exp, 1)
            act.wait_ge(f_exp, 1)
            act.activation(fz[:, 1, :], fz[:, 1, :], ACT.Ln, bias=ones[0:NH, 0:1]).then_inc(f_ln, 1)
            for a in range(4):
                act.wait_ge(ut_mm, a + 1)
                ins = act.activation(ut[:, 4 * a:4 * a + 4, :], quarter(a), ACT.Copy)
            ins.then_inc(ut_out, 1)

            def qk_high_parts(c, j):
                act.wait_ge(evacuated, c * 2 + 2)
                if due(c - 1):
                    act.wait_ge(qk_out[j], c * 16 - (16 * j))
                act.activation(qk_hi[:, j, :], qko[:, j, :], ACT.Copy).then_inc(qk_high, 1)

            def next_split(c, m, j, n):
                ahead(split_high, act, c, m, j)

            def qk_step(c, m, j, n):
                ahead(split_high, act, c, m, j)
                if due(c):
                    qk_high_parts(c - 1, 1 - j)

            steps(act, 0, 4, qk_step, peel=4)
            for a in range(4):
                act.wait_ge(mb_mm, a + 1)
                ins = act.activation(mb[:, a // 2, 4 * (a % 2):4 * (a % 2) + 4, :], quarter(a), ACT.Copy)
            ins.then_inc(mb_out, 1)
            for a in range(4):
                act.wait_ge(kl_mm, a + 1)
                ins = act.activation(kl[0:CH, group_at(a, 0):group_at(a, 3) + 1:2, :],
                                     ps[0:CH, 4 + a, :].rearrange("p (g c) -> p g c", g=4), ACT.Copy)
            ins.then_inc(kl_out, 1)
            steps(act, 4, 8, qk_step, peel=2)
            act.wait_ge(y_sum, 1)
            act.activation(yn[:], yn[:], ACT.Gelu_apprx_tanh).then_inc(gelu_done, 1)
            steps(act, 8, 10, qk_step, peel=2)
            for a in range(4):
                act.wait_ge(gt_mm, a + 1)
                ins = act.activation(gt[:, 4 * a:4 * a + 4, :], quarter(a), ACT.Copy)
            ins.then_inc(gt_out, 1)
            act.wait_ge(glu_sum, 1)
            act.activation(sg[:], sg[:], ACT.Sigmoid).then_inc(glu_sig, 1)
            steps(act, 10, 11, qk_step, peel=1)
            act.wait_ge(y_gated, 1)
            for t in range(TS):
                ins = act.activation(sg[:, t, :], yn[:, t, :], ACT.Square, accum_out=ssy[:, 0, t:t + 1])
            ins.then_inc(y_ssm_sq, 1)
            rsqrt_act(act, nm_norm, ssy[:, 2, 0:NT], ssy[:, 1, 0:NT])
            steps(act, 11, 12, qk_step, peel=1)
            qk_high_parts(11, 1)

            def exp_row(i, j, g, r):
                u = unit(i, j, g)
                if due(piece(i, j, g, 0) - (PCS - g - 1)):
                    act.wait_ge(pt_mm, piece(i, j, g, 0) - (PCS - g - 1))
                if due(u - 3):
                    act.wait_ge(y_done, u - 3)
                act.wait_ge(row_max_done, u * 2 + (r + 1))
                act.activation(probs(g, r), sc[:, r, 0:(g + 1) * QB * P], ACT.Exp, scale=-1.0,
                               bias=nm[:, g, r:r + 1], accum_out=den[:, g, r:r + 1]).then_inc(exp_done, 1)

            def pt_high(i, j, g, b):
                pc, slot = piece(i, j, g, b), slot_of(j, g, b)
                if due(pc - 3):
                    act.wait_ge(pv_done, pc - 3)
                act.wait_ge(pt_mm, pc + 1)
                act.activation(pth[:, slot % 4, :, :], ps[:, 4 + slot % 2, :].rearrange("p (b n) -> p b n", b=2),
                               ACT.Copy).then_inc(pt_high_done, 1)

            def ot_copy(i, j, g):
                if due(unit(i, j, g) - 1):
                    act.wait_ge(yt_mm, unit(i, j, g) - 1)
                act.wait_ge(pv_done, piece(i, j, g, g) + 1)
                act.activation(ot[:, PLACE[g] % 2, :], outputs_bank(g), ACT.Copy).then_inc(ot_done, 1)

            def act_unit(i, j, g, ahead_, prev, on, last):
                if prev:
                    ot_copy(*prev)
                for b in range(max(g + 1, 2)):
                    if b < len(on) and on[b]:
                        pt_high(*on[b])
                    if b < QB and ahead_:
                        exp_row(*ahead_, b)

            for g in ORDER[:2]:
                for r in range(QB):
                    exp_row(0, 0, g, r)
            for n in range(2):
                pt_high(0, *PIECES[n])
            bodies(act, act_unit)
            ot_copy(NH - 1, *BODY[-1])

            def mix_high_part(n):
                k, h = MIX[n]
                act.wait_ge(mix_mm, n + 1)
                act.activation(mix_view(op_hi, k, h), mix_bank(k, n), ACT.Copy,
                               scale=g_sb[:, GAIN_MIX, k:k + 1]).then_inc(mix_high, 1)

            rsqrt_act(act, nm_norm, ssy[:, 2, NT:3 * NT], ssy[:, 1, NT:3 * NT], 2)
            for n in range(4):
                mix_high_part(n)
            act.wait_ge(nm_norm.rstd, 2)
            for h in range(2):
                for m in range(4 * h, 4 * h + 4):
                    part = ya_flat[:, m, ATT_W:2 * ATT_W]
                    ins = act.activation(part, part, ACT.Copy, scale=ssy[:, 2, 2 * NT + m:2 * NT + m + 1])
                ins.then_inc(fox_scaled, 1)
            for n in range(4, MIX_FIRST):
                mix_high_part(n)

            def z_square(squares, sq, h, n, c):
                if n >= 2:
                    act.wait_ge(squares.added, h * (KT - 1) + max(1, n - 2))
                act.wait_ge(evacuated, c * 2 + 2)
                act.activation(sq[:, n % 2, half(h)], z[:, n, half(h)], ACT.Square).then_inc(squares.sq, 1)

            def residual_high(h, k):
                n = h * KT + k
                act.wait_ge(x2_done, n + 1)
                act.activation(op_hi[:, k, half(h)], x2[:, k, half(h)], ACT.Copy,
                               scale=g_sb[:, GAIN_FFN_PRE, k:k + 1]).then_inc(h2_high, 1)
                if n >= 2:
                    act.wait_ge(h2_squares.added, n - 1)
                act.activation(sq2b[:, n % 2, :], x2[:, k, half(h)], ACT.Square).then_inc(h2_squares.sq, 1)

            for n in range(2 * KT):
                c = C_OUT + n
                ahead(split_high, act, c, c // 2, c % 2)
                if n == 0:
                    for i in range(MIX_FIRST, len(MIX)):
                        mix_high_part(i)
                if n >= KT + 2:
                    residual_high(0, n - KT - 2)
                if n:
                    z_square(zo_squares, sq2, (n - 1) // KT, (n - 1) % KT, c - 1)
                if n == KT:
                    rsqrt_act(act, no_norm, rb[:, half(0)], n2[:, 0, half(0)])
            z_square(zo_squares, sq2, 1, KT - 1, C_FFN - 1)
            residual_high(0, KT - 2)
            split_high(act, C_FFN + 1, (C_FFN + 1) // 2, 1)
            residual_high(0, KT - 1)
            rsqrt_act(act, no_norm, rb[:, half(1)], n2[:, 0, half(1)], 2)
            rsqrt_act(act, nf_norm, nf_rstd[:], n2[:, 1, half(0)])
            for k in range(KT):
                residual_high(1, k)

            def silu(h, count):
                act.wait_ge(evacuated, count)
                act.activation(tg[:, half(h)], tg[:, half(h)], ACT.Silu).then_inc(silu_done, 1)

            def hidden_high(f, i, h):
                act.wait_ge(hf_done, f * 2 + (h + 1))
                act.wait_ge(x2_out, 16 * 2)
                act.activation(hid_hi[:, i, half(h)], hf[:, half(h)], ACT.Copy).then_inc(hid_high, 1)

            silu(0, 2 * C_FFN + 1)
            act.wait_ge(mm_done, 2 * C_FFN + 3)
            split_high(act, C_FFN + 2, (C_FFN + 2) // 2, 0)
            hidden_high(0, 0, 0)
            rsqrt_act(act, nf_norm, rb[:, half(1)], n2[:, 0, half(1)], 2)
            silu(1, 2 * C_FFN + 3)
            hidden_high(0, 0, 1)

            def gate_up(m0, f0):
                def step(c, m, j, n):
                    ahead(split_high, act, c, m, j)
                    f = m - (m0 - f0)
                    for h in range(2):
                        if j == 0:
                            silu(h, c * 2 + (h + 1))
                        else:
                            hidden_high(f, m - m0, h)
                return step

            for p_ in range(len(PARTS)):
                gu, dn = BASES[p_]
                steps(act, gu + (2 if p_ == 0 else 0), dn, gate_up(gu // 2, sum(PARTS[:p_])))
                if p_ < len(PARTS) - 1:
                    steps(act, dn, dn + KT, next_split)
            for n in range(2 * KT):
                c = BASES[-1][1] + n
                if c + 1 < C_END:
                    ahead(split_high, act, c, c // 2, c % 2)
                if n:
                    z_square(ff_squares, r1["sq3"], (n - 1) // KT, (n - 1) % KT, c - 1)
                if n == KT + 1:
                    rsqrt_act(act, ne_norm, rb[:, half(0)], r1["n3"][:, 0, half(0)])
            z_square(ff_squares, r1["sq3"], 1, KT - 1, C_END - 1)
            rsqrt_act(act, ne_norm, rb[:, half(1)], r1["n3"][:, 0, half(1)], 2)
            for k in range(OUT_DVE, KT):
                act.activation(z[:, k, half(1)], z[:, k, half(1)], ACT.Copy,
                               scale=g_sb[:, GAIN_FFN_POST, k:k + 1]).then_inc(z_gained, 1)

        @block.vector
        def _(dve):
            chain = [0]

            def link(ins):
                chain[0] += 1
                ins.then_inc(dve_chain, 1)
                dve.wait_ge(dve_chain, chain[0])

            def tt(out, a, b, op):
                return dve.tensor_tensor(out, a, b, op)

            def cmul(o_re, o_im, a_re, a_im, b_re, b_im, t1, t2):
                tt(t1, a_re, b_re, ALU.mult)
                link(tt(t2, a_im, b_im, ALU.mult))
                link(tt(o_re, t1, t2, ALU.subtract))
                tt(t1, a_re, b_im, ALU.mult)
                link(tt(t2, a_im, b_re, ALU.mult))
                link(tt(o_im, t1, t2, ALU.add))

            dve.memset(ones[:], 1.0).then_inc(ones_set, 1)

            def decay_and_angle():
                dve.wait_ge(par_act, 1)
                link(tt(q(ARDT), q(AR), q(DT), ALU.mult))
                tt(q(TH), q(AI), q(DT), ALU.mult).then_inc(par_dve, 1)

            def reduced_angle():
                dve.wait_ge(par_dve, 1)
                magic = 12582912.0
                link(dve.tensor_scalar(q(KR), q(TH), 1.0 / (2 * math.pi), magic, ALU.mult, ALU.add))
                link(dve.tensor_scalar(q(KR), q(KR), magic, None, ALU.subtract))
                c1 = 6.28125
                c2 = float((np.float32(2 * math.pi - c1).view(np.uint32) & np.uint32(0xFFFFE000)).view(np.float32))
                c3 = 2 * math.pi - c1 - c2
                link(dve.scalar_tensor_tensor(out=q(RR), in0=q(KR), scalar=-c1, in1=q(TH), op0=ALU.mult, op1=ALU.add))
                link(dve.scalar_tensor_tensor(out=q(RR), in0=q(KR), scalar=-c2, in1=q(RR), op0=ALU.mult, op1=ALU.add))
                link(dve.scalar_tensor_tensor(out=q(RR), in0=q(KR), scalar=-c3, in1=q(RR), op0=ALU.mult, op1=ALU.add))
                pi = 3.1415925
                dve.tensor_scalar(q(RR), q(RR), pi, -pi, ALU.min, ALU.max).then_inc(par_dve, 1)

            def coefficient():
                dve.wait_ge(par_act, 3)
                link(tt(q(CS), q(SH), q(SH), ALU.mult))
                link(dve.tensor_scalar(q(CS), q(CS), -2.0, 1.0, ALU.mult, ALU.add))
                link(tt(q(ABR), q(DEC), q(CS), ALU.mult))
                link(tt(q(ABI), q(DEC), q(SN), ALU.mult))
                dve.tensor_scalar(q(M1), q(ABR), -1.0, None, ALU.add)
                tt(q(MAG), q(AR), q(AR), ALU.mult)
                link(tt(q(TA), q(AI), q(AI), ALU.mult))
                link(tt(q(MAG), q(MAG), q(TA), ALU.add))
                link(dve.reciprocal(q(MAG), q(MAG)))
                tt(q(CR), q(M1), q(AR), ALU.mult)
                link(tt(q(TA), q(ABI), q(AI), ALU.mult))
                link(tt(q(CR), q(CR), q(TA), ALU.add))
                link(tt(q(CR), q(CR), q(MAG), ALU.mult))
                tt(q(CI), q(ABI), q(AR), ALU.mult)
                link(tt(q(TA), q(M1), q(AI), ALU.mult))
                link(tt(q(CI), q(CI), q(TA), ALU.subtract))
                link(tt(q(CI), q(CI), q(MAG), ALU.mult))

            def input_matrix():
                dve.wait_ge(bc_in, 16)
                cr = q(CR).unsqueeze(2).to_broadcast((P, NJ, CH))
                ci = q(CI).unsqueeze(2).to_broadcast((P, NJ, CH))
                cmul(bbar[:, 0], bbar[:, 1], cr, ci, bc[:, 0], bc[:, 1], tb[:, 0], tb[:, 1])
                dve.tensor_scalar(tb[:, 0], bc[:, 2], -1.0, None, ALU.mult)
                dve.tensor_scalar(tb[:, 1], bc[:, 3], -1.0, None, ALU.mult)

            def abar_powers():
                dve.memset(pw[:, 0, 0, :], 1.0)
                dve.memset(pw[:, 1, 0, :], 0.0)
                dve.tensor_copy(pw[:, 0, 1, :], q(ABR))
                link(dve.tensor_copy(pw[:, 1, 1, :], q(ABI)))
                n = 1
                while n < TS:
                    hi = slice(n + 1, 2 * n + 1)
                    lo = slice(1, n + 1)
                    a_re, a_im = (pw[:, r, lo, :] for r in range(2))
                    b_re, b_im = (pw[:, r, n:n + 1, :].to_broadcast((P, n, NJ)) for r in range(2))
                    t1 = ssy_flat[:, 0:n * NJ].rearrange("p (l j) -> p l j", j=NJ)
                    t2 = ssy_flat[:, TS // 2 * NJ:TS // 2 * NJ + n * NJ].rearrange("p (l j) -> p l j", j=NJ)
                    cmul(pw[:, 0, hi, :], pw[:, 1, hi, :], a_re, a_im, b_re, b_im, t1, t2)
                    n *= 2
                for n in range(TS):
                    dve.tensor_copy(pw_back[:, :, TS - 1 - n, :], pw[:, :, n, :])

            def chunk_rotations():
                dve.tensor_copy(wp[:, 0, 7, :], q(CS))
                link(dve.tensor_copy(wp[:, 1, 7, :], q(SN)))
                src = 7
                squarings = [7, 7, 0] + list(range(1, 7))
                for dst in squarings:
                    cmul(q(T1), q(T2), wp[:, 0, src], wp[:, 1, src], wp[:, 0, src], wp[:, 1, src], q(TA), q(TB_))
                    dve.tensor_copy(wp[:, 0, dst, :], q(T1))
                    link(dve.tensor_copy(wp[:, 1, dst, :], q(T2)))
                    src = dst
                dve.tensor_copy(q(TC), q(T1)).then_inc(powers, 1)

            between = {1: decay_and_angle, 2: reduced_angle, 7: coefficient}
            dve.wait_ge(gains_in, 16)
            for k in range(KT):
                dve.wait_ge(x_high, k + 1)
                dve.scalar_tensor_tensor(out=op_lo[:, k, :], in0=xt[:, k, :], scalar=g_sb[:, GAIN_PRE, k:k + 1],
                                         in1=op_hi[:, k, :].bitcast(f32), op0=ALU.mult,
                                         op1=ALU.subtract).then_inc(x_split, 1)
                if k % 2 == 0:
                    dve.wait_ge(uf_high, k // 2 + 1)
                    tt(ufl[:, k:k + 2, :], uf_raw[:, k:k + 2, :], ufh[:, k:k + 2, :].bitcast(f32),
                       ALU.subtract).then_inc(uf_split, 1)
                if k in between:
                    between[k]()

            def v_low(w):
                dve.wait_ge(v_high_done, w + 1)
                tt(vl[:, w % 2, :, :], v_raw, vh[:, w % 2, :, :].bitcast(f32), ALU.subtract).then_inc(v_split, 1)

            v_low(0)
            input_matrix()
            dve.wait_ge(n1s_norm.sums, 1)
            rsqrt_in(dve, n1s_norm, rn[:, 1, :], ps[:, 2, 0:2 * NT], D)
            rsqrt_out(dve, link, n1s_norm, rn[:, 0, :], rn[:, 1, :], rn[:, 2, :])
            v_low(1)
            abar_powers()
            dve.wait_ge(n1_norm.sums, 2)
            rsqrt_in(dve, n1_norm, n1[:, 0, :], ps[:, 0:2, :].rearrange("p b n -> p (b n)"), D)
            rsqrt_out(dve, link, n1_norm, rb[:], n1[:, 0, :], n1[:, 1, :])
            chunk_rotations()
            v_low(2)
            dve.wait_ge(n1s_norm.rstd, 1)
            dve.wait_ge(uf_copied, 1 + TS)
            rs = rn[:, 0, NT:2 * NT]
            tt(fl[:], fl[:], rs.unsqueeze(2).to_broadcast((P, TS, NH)), ALU.mult)
            tt(ug[:], ug[:], rs.unsqueeze(1).unsqueeze(3).to_broadcast((P, G, TS, CH)),
               ALU.mult).then_inc(uf_scaled, 1)
            split_low(dve, 0, 0, 0)
            dve.wait_ge(f_mm, 1)
            dve.wait_ge(bf_in, 16)
            f_in = ps[0:NH, 2:4, :].rearrange("p b n -> p (b n)").rearrange("p (s c) -> p c s", s=TS)
            link(dve.tensor_scalar(fz[:, 0, :].rearrange("p (c s) -> p c s", s=TS), f_in, bfs[:, 0:1], None, ALU.add))
            dve.scalar_tensor_tensor(out=fz[:, 1, :], in0=fz[:, 0, :], scalar=-1.0, in1=fz[:, 0, :], op0=ALU.mult,
                                     op1=ALU.min).then_inc(f_abs, 1)
            shape = (P, NJ, TS, CH)
            a_re, a_im = (pw_back[:, r].rearrange("p l j -> p j l").unsqueeze(3).to_broadcast(shape) for r in range(2))
            b_re, b_im = (bbar[:, r].unsqueeze(2).to_broadcast(shape) for r in range(2))
            m_re, m_im = (mt[:, r].rearrange("p j (s c) -> p j s c", s=TS) for r in range(2))
            u1, u2 = (hs[:, r].rearrange("p j (s c) -> p j s c", s=TS) for r in range(2))

            def evacuate_qk(c, m, j):
                if due(m * 32):
                    dve.wait_ge(qk_out[j], m * 32)
                for h in range(2):
                    dve.wait_ge(mm_done, c * 2 + (h + 1))
                    dve.scalar_tensor_tensor(out=qko[:, j, half(h)], in0=ps[:, 2 * j + h, :],
                                             scalar=DH ** -0.5 if j == 0 else 1.0, in1=rb[:, half(h)],
                                             op0=ALU.mult, op1=ALU.mult).then_inc(evacuated, 1)

            def qk_step(c, m, j, n):
                ahead(split_low, dve, c, m, j)
                evacuate_qk(c, m, j)

            ahead(split_low, dve, 0, 0, 0)
            dve.wait_ge(v_out, 16 * 4 * NV)
            dve.wait_ge(v_mm, NV * NT)
            tt(u1, a_re, b_re, ALU.mult)
            link(tt(u2, a_im, b_im, ALU.mult))
            link(tt(m_re, u1, u2, ALU.subtract))
            evacuate_qk(0, 0, 0)
            ahead(split_low, dve, 1, 0, 1)
            tt(u1, a_re, b_im, ALU.mult)
            link(tt(u2, a_im, b_re, ALU.mult))
            tt(m_im, u1, u2, ALU.add).then_inc(mt_done, 1)
            evacuate_qk(1, 0, 1)
            qk_step(2, 1, 0, 2)
            dve.wait_ge(f_ln, 1)
            link(dve.tensor_scalar(fz[:, 0, :], fz[:, 0, :], 0.0, None, ALU.min))
            link(tt(fz[:, 1, :], fz[:, 1, :], fz[:, 0, :], ALU.subtract))
            dve.tensor_tensor_scan(out=fz[:, 0, :], data0=ones[0:NH, 0:1].to_broadcast((NH, SEQ)), data1=fz[:, 1, :],
                                   initial=0.0, op0=ALU.mult, op1=ALU.add).then_inc(f_cum, 1)

            qk_step(3, 1, 1, 3)
            ahead(split_low, dve, 4, 2, 0)
            dve.wait_ge(x_mm, 1)
            dve.wait_ge(e_done, 1)
            x_re, x_im = (ps[:, 4 + 2 * r:6 + 2 * r, :].rearrange("p b (j c) -> p (b j) c", c=NC) for r in range(2))
            t1, t2 = (pt[:, r, :, 0:NC] for r in range(2))
            z_re, z_im = mt[:, 0], mt[:, 1]
            tt(t1, x_re, ere[:], ALU.mult)
            link(tt(t2, x_im, eim[:], ALU.mult))
            link(tt(z_re, t1, t2, ALU.add))
            tt(t1, x_im, ere[:], ALU.mult)
            link(tt(t2, x_re, eim[:], ALU.mult))
            link(tt(z_im, t1, t2, ALU.subtract))
            for r in range(2):
                for j in range(NJ):
                    ins = dve.tensor_tensor_scan(out=ss[:, r, j, :], data0=sp[:, RHO, j:j + 1].to_broadcast((P, NC)),
                                                 data1=mt[:, r, j, :], initial=0.0, op0=ALU.mult, op1=ALU.add)
            link(ins)
            evacuate_qk(4, 2, 0)
            ahead(split_low, dve, 5, 2, 1)
            dve.wait_ge(tz_in, 16 * TS)
            dve.memset(hs[:, :, :, 0:1], 0.0)
            cut = slice(0, NC - 1)
            cmul(hs[:, 0, :, 1:NC], hs[:, 1, :, 1:NC], ss[:, 0, :, cut], ss[:, 1, :, cut],
                 ere[:, :, cut], eim[:, :, cut], t1[:, :, cut], t2[:, :, cut])
            dve.tensor_copy(q(TC), q(T1)).then_inc(h_done, 1)
            evacuate_qk(5, 2, 1)
            steps(dve, 6, 8, qk_step)
            dve.wait_ge(y_mm, 1)
            dve.wait_ge(du_done, 1)
            for g in range(G):
                a, b = bank_of(g)
                y = ps[:, 4 + a, b * P:(b + 1) * P].rearrange("p (t o) -> p t o", t=TS)
                ins = tt(yn[:, :, g * CH:(g + 1) * CH], y, ug[:, g], ALU.add)
            ins.then_inc(y_sum, 1)
            steps(dve, 8, 10, qk_step, peel=2)
            dve.wait_ge(glu_mm, 1)
            tt(sg[:], ps[:, 4:8, :].rearrange("p b (t n) -> p (b t) n", t=2),
               row[:, 1:2, :].to_broadcast((P, TS, SSM_W)), ALU.add).then_inc(glu_sum, 1)
            dve.wait_ge(glu_sig, 1)
            tt(yn[:], yn[:], sg[:], ALU.mult).then_inc(y_gated, 1)

            qk_step(10, 5, 0, 10)
            dve.wait_ge(y_ssm_sq, 1)
            rsqrt_in(dve, nm_norm, ssy[:, 1, 0:NT], ssy[:, 0, 0:NT], SSM_W)
            ahead(split_low, dve, 11, 5, 1)
            rsqrt_out(dve, link, nm_norm, ssy[:, 2, 0:NT], ssy[:, 1, 0:NT], ssy[:, 3, 0:NT])
            dve.wait_ge(nm_norm.rstd, 1)
            tt(yn[:], yn[:], ssy[:, 2, 0:NT].unsqueeze(2).to_broadcast((P, TS, SSM_W)),
               ALU.mult).then_inc(y_scaled, 1)
            evacuate_qk(11, 5, 1)

            def values_high(i, j):
                hc = i * 2 + j
                if due(hc * PCS - PCS):
                    dve.wait_ge(pv_done, hc * PCS - PCS)
                dve.wait_ge(values_in[j], i * 16 + 16)
                dve.tensor_copy(vs[:, j, :, 0:DH], vv[:, j, :, :]).then_inc(values_high_done, 1)

            def row_max(i, j, g, r):
                u, w = unit(i, j, g), (g + 1) * QB * P
                dve.wait_ge(qk_done, u * 2 + (r + 1))
                if due(u * 2 + (r - 1)):
                    dve.wait_ge(exp_done, u * 2 + (r - 1))
                if j == 0:
                    off = SEQ - P - P * (QB * g + r)
                    bias = lnc[:, off:off + w]
                else:
                    dve.wait_ge(fb_in, i * 16 + 16)
                    bias = fb[:, 0:w]
                dve.wait_ge(lnc_in, 16)
                dve.sem_inc(dve_waited, 1)
                scores = ps[:, 2 * r:2 * r + 2, :].rearrange("p b n -> p (b n)")
                dve.tensor_tensor_reduce(out=sc[:, r, 0:w], in0=scores[:, 0:w], in1=bias,
                                         scale=-1.0, scalar=3e38, op0=ALU.add, op1=ALU.min,
                                         accum_out=nm[:, g, r:r + 1]).then_inc(row_max_done, 1)

            def pt_low(i, j, g, b):
                pc, slot = piece(i, j, g, b), slot_of(j, g, b)
                dve.wait_ge(pt_high_done, pc + 1)
                tt(ptl[:, slot % 4, :, :], ps[:, 4 + slot % 2, :].rearrange("p (b n) -> p b n", b=2),
                   pth[:, slot % 4, :, :].bitcast(f32), ALU.subtract).then_inc(pt_low_done, 1)

            def sum_inverse(i, j, g):
                dve.wait_ge(exp_done, unit(i, j, g) * 2 + 2)
                dve.reciprocal(rden[:, PLACE[g] % 2, :], den[:, g, :]).then_inc(rden_done, 1)

            def y_unit(i, j, g):
                u = unit(i, j, g)
                dve.wait_ge(yt_mm, u + 1)
                dve.wait_ge(rden_done, u + 1)
                tt(ya[:, QB * g:QB * (g + 1), i + NH * j, :],
                   ps[:, 6 + PLACE[g] % 2, QB * P:QB * P + QB * DH].rearrange("p (r d) -> p r d", r=QB),
                   rden[:, PLACE[g] % 2, :].unsqueeze(2).to_broadcast((P, QB, DH)), ALU.mult).then_inc(y_done, 1)

            def dve_unit(i, j, g, ahead_, prev, on, last):
                if prev:
                    sum_inverse(*prev)
                for b in range(max(g + 1, 2)):
                    if b < QB and ahead_:
                        row_max(*ahead_, b)
                    if b < len(on) and on[b]:
                        pt_low(*on[b])
                    if b == 1 and prev:
                        y_unit(*prev)
                if g == ORDER[0] and not (last and j == 1):
                    values_high(*((i, 1) if j == 0 else (i + 1, 0)))

            values_high(0, 0)
            for g in ORDER[:2]:
                for r in range(QB):
                    row_max(0, 0, g, r)
            for n in range(2):
                pt_low(0, *PIECES[n])
            for j in range(2):
                dve.wait_ge(qk_out[j], 2 * 16 * NH)
            bodies(dve, dve_unit)
            sum_inverse(NH - 1, *BODY[-1])
            dve.wait_ge(y_att_sq, 2 * (2 * NH - 1))
            dve.tensor_reduce(ssy[:, 0, NT:2 * NT], y_sq_sum[:, 0], AX.X, ALU.add)
            y_unit(NH - 1, *BODY[-1])

            dve.wait_ge(y_done, 2 * NH * UNITS)
            last_y = ya[:, :, 2 * NH - 1, :]
            link(tt(y_sq[:, 1], last_y, last_y, ALU.mult))
            link(tt(y_sq_sum[:, 1], y_sq_sum[:, 1], y_sq[:, 1], ALU.add))
            link(dve.tensor_reduce(ssy[:, 0, 2 * NT:3 * NT], y_sq_sum[:, 1], AX.X, ALU.add))
            rsqrt_in(dve, nm_norm, ssy[:, 1, NT:3 * NT], ssy[:, 0, NT:3 * NT], ATT_W)

            def mix_low_part(n):
                k, h = MIX[n]
                dve.wait_ge(mix_high, n + 1)
                dve.scalar_tensor_tensor(out=mix_view(op_lo, k, h), in0=mix_bank(k, n),
                                         scalar=g_sb[:, GAIN_MIX, k:k + 1], in1=mix_view(op_hi, k, h).bitcast(f32),
                                         op0=ALU.mult, op1=ALU.subtract).then_inc(mix_split, 1)

            rsqrt_out(dve, link, nm_norm, ssy[:, 2, NT:3 * NT], ssy[:, 1, NT:3 * NT], ssy[:, 3, NT:3 * NT], 2)
            dve.wait_ge(nm_norm.rstd, 2)
            for h in range(2):
                m = slice(4 * h, 4 * h + 4)
                tt(ya_flat[:, m, 0:ATT_W], ya_flat[:, m, 0:ATT_W],
                   ssy[:, 2, NT + 4 * h:NT + 4 * h + 4].unsqueeze(2).to_broadcast((P, 4, ATT_W)),
                   ALU.mult).then_inc(y_scaled, 1)
                if h == 0:
                    for n in range(4):
                        mix_low_part(n)
            for n in range(4, MIX_FIRST):
                mix_low_part(n)

            def norm_in(norm, h, out, bank):
                dve.wait_ge(norm.sums, h + 1)
                rsqrt_in(dve, norm, out, ps[:, bank, :], D)

            joined = [0]

            def residual_tiles(h, tiles):
                for k in tiles:
                    tt(z[:, k, half(h)], z[:, k, half(h)], rb[:, half(h)], ALU.mult).then_inc(zn, 1)
                    joined[0] += 1
                    if k > 0:
                        residual_low(joined[0] - 2)
                    dve.wait_ge(zn, joined[0])
                    if h == 0:
                        dve.wait_ge(x_in[k], 32)
                    dve.scalar_tensor_tensor(out=x2[:, k, half(h)], in0=z[:, k, half(h)],
                                             scalar=g_sb[:, GAIN_POST, k:k + 1], in1=x2[:, k, half(h)],
                                             op0=ALU.mult, op1=ALU.add).then_inc(x2_done, 1)

            def residual_low(n):
                h, k = n // KT, n % KT
                dve.wait_ge(h2_high, n + 1)
                dve.scalar_tensor_tensor(out=op_lo[:, k, half(h)], in0=x2[:, k, half(h)],
                                         scalar=g_sb[:, GAIN_FFN_PRE, k:k + 1],
                                         in1=op_hi[:, k, half(h)].bitcast(f32), op0=ALU.mult,
                                         op1=ALU.subtract).then_inc(h2_split, 1)

            for h in range(2):
                for n in range(KT):
                    c = C_OUT + h * KT + n
                    ahead(split_low, dve, c, c // 2, c % 2)
                    if h == 0 and n == 0:
                        for i in range(MIX_FIRST, len(MIX)):
                            mix_low_part(i)
                    if h == 1 and n == 0:
                        norm_in(no_norm, 0, n2[:, 0, half(0)], 4)
                    if h == 1 and n == 1:
                        rsqrt_out(dve, link, no_norm, rb[:, half(0)], n2[:, 0, half(0)], n2[:, 1, half(0)])
                        dve.wait_ge(no_norm.rstd, 1)
                    if h == 1 and n:
                        residual_tiles(0, (n - 1,))
                    dve.wait_ge(mm_done, c * 2 + 2)
                    dve.tensor_copy(z[:, n, half(h)], ps[:, 2 * (c % 2), :]).then_inc(evacuated, 2)
            residual_tiles(0, (KT - 1,))
            split_low(dve, C_FFN + 1, (C_FFN + 1) // 2, 1)
            residual_low(KT - 1)
            norm_in(no_norm, 1, n2[:, 0, half(1)], 5)
            norm_in(nf_norm, 0, n2[:, 1, half(0)], 6)
            rsqrt_out(dve, link, no_norm, rb[:, half(1)], n2[:, 0, half(1)], n2[:, 1, half(1)], 2)
            dve.wait_ge(no_norm.rstd, 2)
            residual_tiles(1, range(KT))
            residual_low(2 * KT - 1)
            rsqrt_out(dve, link, nf_norm, nf_rstd[:], n2[:, 1, half(0)], n2[:, 1, half(1)])
            dve.wait_ge(nf_norm.rstd, 1)

            def gate_or_up(c, m, j, h, count, scale):
                dve.wait_ge(mm_done, count)
                tt((tg if j == 0 else hf)[:, half(h)], ps[:, 2 * j + h, :], scale, ALU.mult).then_inc(evacuated, 1)

            def hidden(f, h, count):
                dve.wait_ge(silu_done, f * 2 + (h + 1))
                dve.wait_ge(evacuated, count)
                tt(hf[:, half(h)], hf[:, half(h)], tg[:, half(h)], ALU.mult).then_inc(hf_done, 1)

            for j in range(2):
                gate_or_up(C_FFN + j, C_FFN // 2, j, 0, 2 * C_FFN + 1 + j, nf_rstd[:])
            norm_in(nf_norm, 1, n2[:, 0, half(1)], 7)
            split_low(dve, C_FFN + 2, (C_FFN + 2) // 2, 0)
            hidden(0, 0, 2 * C_FFN + 2)
            dve.tensor_copy(rb[:, half(0)], nf_rstd[:])
            rsqrt_out(dve, link, nf_norm, rb[:, half(1)], n2[:, 0, half(1)], n2[:, 1, half(1)], 2)
            dve.wait_ge(nf_norm.rstd, 2)
            for j in range(2):
                gate_or_up(C_FFN + j, C_FFN // 2, j, 1, 2 * C_FFN + 3 + j, rb[:, half(1)])
            hidden(0, 1, 2 * C_FFN + 4)

            def gate_up(p_, gu):
                def step(c, m, j, n):
                    f = m - (gu // 2 - sum(PARTS[:p_]))
                    ahead(split_low, dve, c, m, j)
                    for h in range(2):
                        if j == 1:
                            dve.wait_ge(hid_low, f * 2 + (h - 1))
                        gate_or_up(c, m, j, h, c * 2 + (h + 1), rb[:, half(h)])
                    if j == 1:
                        for h in range(2):
                            hidden(f, h, c * 2 + (h + 1))
                return step

            def down(p_):
                def step(c, m, j, n):
                    ahead(split_low, dve, c, m, j)
                    for h in range(2):
                        dve.wait_ge(mm_done, c * 2 + (h + 1))
                        dve.wait_ge(gains_in, 16)
                        if p_ == 0:
                            ins = dve.tensor_copy(z[:, n, half(h)], ps[:, 2 * j + h, :])
                        else:
                            ins = tt(z[:, n, half(h)], ps[:, 2 * j + h, :], z[:, n, half(h)], ALU.add)
                        ins.then_inc(evacuated, 1)
                return step

            for p_ in range(len(PARTS)):
                gu, dn = BASES[p_]
                steps(dve, gu + (2 if p_ == 0 else 0), dn, gate_up(p_, gu))
                if p_ < len(PARTS) - 1:
                    steps(dve, dn, dn + KT, down(p_))

            results = [0]

            def result_tiles(h, tiles):
                for k in tiles:
                    results[0] += 1
                    tt(z[:, k, half(h)], z[:, k, half(h)], rb[:, half(h)], ALU.mult).then_inc(ze, 1)
                    dve.wait_ge(ze, results[0])
                    dve.wait_ge(x2_again, 16 * (k + 1))
                    dve.scalar_tensor_tensor(out=z[:, k, half(h)], in0=z[:, k, half(h)],
                                             scalar=g_sb[:, GAIN_FFN_POST, k:k + 1], in1=r1["x2r"][:, k, half(h)],
                                             op0=ALU.mult, op1=ALU.add).then_inc(out_done, 1)

            n3 = r1["n3"]
            for h in range(2):
                for n in range(KT):
                    c = BASES[-1][1] + h * KT + n
                    if c + 1 < C_END:
                        ahead(split_low, dve, c, c // 2, c % 2)
                    if h == 1 and n == 2:
                        rsqrt_out(dve, link, ne_norm, rb[:, half(0)], n3[:, 0, half(0)], n3[:, 1, half(0)])
                        dve.wait_ge(ne_norm.rstd, 1)
                    if h == 1:
                        result_tiles(0, OUT_TILES[n])
                    dve.wait_ge(mm_done, c * 2 + 2)
                    tt(z[:, n, half(h)], ps[:, 2 * (c % 2), :], z[:, n, half(h)], ALU.add).then_inc(evacuated, 2)
                    if h == 1 and n == 0:
                        norm_in(ne_norm, 0, n3[:, 0, half(0)], 4)
            norm_in(ne_norm, 1, n3[:, 0, half(1)], 5)
            result_tiles(0, (6, 7))
            rsqrt_out(dve, link, ne_norm, rb[:, half(1)], n3[:, 0, half(1)], n3[:, 1, half(1)], 2)
            dve.wait_ge(ne_norm.rstd, 2)
            result_tiles(1, range(OUT_DVE))

        @block.gpsimd
        def _(pool):
            chain = [0]

            def link(ins):
                chain[0] += 1
                ins.then_inc(pool_chain, 1)
                pool.wait_ge(pool_chain, chain[0])

            def tt(out, a, b, op):
                return pool.tensor_tensor(out, a, b, op)

            pool.memset(ident_b[:], 0.0)
            pool.memset(mask_b[:], 0.0)
            pool.memset(ident2[:], 0.0)
            link(pool.memset(ident[:], 0.0))
            for b in range(2):
                pool.affine_select(out=ident2[:], in_=ident2[:], compare_op=ALU.not_equal, fill=1.0, base=-DH * b,
                                   pattern=[[-1, DH]], channel_multiplier=1).then_inc(ident2_set, 1)
                pool.wait_ge(ident2_set, b + 1)
            for t in (ident, ident_b):
                pool.affine_select(out=t[:], in_=t[:], compare_op=ALU.not_equal, fill=1.0, base=0,
                                   pattern=[[-1, P]], channel_multiplier=1)
            pool.affine_select(out=mask_b[:], in_=mask_b[:], compare_op=ALU.is_ge, fill=MASKED, base=0,
                               pattern=[[P, QB], [-1, QB * P]], channel_multiplier=1).then_inc(ident_set, 1)
            pool.wait_ge(sq_x, 2)
            tt(acc1[:], sq1[:, 0, :], sq1[:, 1, :], ALU.add).then_inc(sq_added, 1)
            for k in range(2, KT):
                pool.wait_ge(sq_x, k + 1)
                pool.wait_ge(sq_added, k - 1)
                tt(acc1[:], acc1[:], sq1[:, k % 2, :], ALU.add).then_inc(sq_added, 1)

            pool.wait_ge(uf_mm, 1)
            pool.wait_ge(n1_norm.sums, 2)
            pool.wait_ge(powers, 1)
            shape = (P, NJ, TS + 1, CH)
            p_re, p_im = (pw[:, r].rearrange("p l j -> p j l") for r in range(2))
            t1, t2 = (pt[:, r].rearrange("p j (l o) -> p j l o", o=CH) for r in range(2))

            for l_ in range(TS + 1):
                pr_ = p_re[:, :, l_:l_ + 1].to_broadcast((P, NJ, CH))
                pi_ = p_im[:, :, l_:l_ + 1].to_broadcast((P, NJ, CH))
                tt(t1[:, :, l_], bc[:, 2], pr_, ALU.mult)
                tt(t2[:, :, l_], bc[:, 3], pi_, ALU.mult)
            link(pool.memset(ere[:, :, 0:1], 1.0))
            link(tt(dre[:].rearrange("p j l o -> p (j l o)"), pt[:, 0].rearrange("p j n -> p (j n)"),
                    pt[:, 1].rearrange("p j n -> p (j n)"), ALU.subtract))
            for l_ in range(TS + 1):
                pr_ = p_re[:, :, l_:l_ + 1].to_broadcast((P, NJ, CH))
                pi_ = p_im[:, :, l_:l_ + 1].to_broadcast((P, NJ, CH))
                tt(t1[:, :, l_], tb[:, 0], pi_, ALU.mult)
                tt(t2[:, :, l_], tb[:, 1], pr_, ALU.mult)
            link(pool.memset(eim[:, :, 0:1], 0.0))
            link(tt(dim_[:].rearrange("p j l o -> p (j l o)"), pt[:, 0].rearrange("p j n -> p (j n)"),
                    pt[:, 1].rearrange("p j n -> p (j n)"), ALU.add))
            pool.memset(pt[:, 0, 0:1, 0:1], 0.0).then_inc(d_done, 1)
            pool.wait_ge(d_done, 1)
            for b in range(7):
                n = 1 << b
                lo, hi = slice(0, n), slice(n, 2 * n)
                w_re, w_im = (wp[:, r, b, :].unsqueeze(2).to_broadcast((P, NJ, n)) for r in range(2))
                s1, s2 = (pt[:, r, :, 0:n] for r in range(2))
                s3, s4 = (pt[:, r, :, 64:64 + n] for r in range(2))
                tt(s1, ere[:, :, lo], w_re, ALU.mult)
                tt(s2, eim[:, :, lo], w_im, ALU.mult)
                tt(s3, ere[:, :, lo], w_im, ALU.mult)
                link(tt(s4, eim[:, :, lo], w_re, ALU.mult))
                tt(ere[:, :, hi], s1, s2, ALU.subtract)
                link(tt(eim[:, :, hi], s3, s4, ALU.add))
            pool.memset(pt[:, 0, 0:1, 0:1], 0.0).then_inc(e_done, 1)
            pool.wait_ge(v_mm, NV * NT)
            pool.dma_start(wg[:], w_glu).then_inc(wg_in, 16)
            pool.dma_start(row[:], rows.partition_broadcast(P)).then_inc(row_in, 16)
            pool.memset(tz[:], 0.0).then_inc(tz_zero, 1)
            pool.wait_ge(row_in, 16)
            pool.wait_ge(ut_out, 1)
            for t in range(TS):
                ins = tt(ug[:, :, t, :], ug[:, :, t, :], row[:, 0, :].rearrange("p (g c) -> p g c", c=CH), ALU.mult)
            ins.then_inc(du_done, 1)

            def qk_low_parts(c, j):
                pool.wait_ge(qk_high, c + 1)
                tt(qk_lo[:, j, :], qko[:, j, :], qk_hi[:, j, :].bitcast(f32), ALU.subtract).then_inc(qk_low, 1)

            for c in range(2):
                qk_low_parts(c, c % 2)
            pool.wait_ge(f_cum, 1)
            pool.dma_start(cum_dram, fz[:, 0, :]).then_inc(cum_out, 16)
            qk_low_parts(2, 0)
            pool.wait_ge(kl_out, 1)
            pool.wait_ge(tz_zero, 1)
            for s in range(TS):
                pool.dma_start(tz[CH * s:CH * (s + 1), :, CH * s:P], kl[0:CH, :, 0:P - CH * s]).then_inc(tz_in, 16)

            with pool.Fori(0, 3) as i:
                for j in range(2):
                    qk_low_parts(i * 2 + (3 + j), 1 - j)
            qk_low_parts(9, 1)

            def head_squares(i, j):
                hc = i * 2 + j
                pool.wait_ge(y_done, hc * UNITS + UNITS)
                if due(hc * 2):
                    pool.wait_ge(y_att_sq, hc * 2)
                pool.wait_ge(gains_in, 16)
                y = ya[:, :, i + NH * j, :]
                tt(y_sq[:, j], y, y, ALU.mult).then_inc(y_att_sq, 1)
                pool.wait_ge(y_att_sq, hc * 2 + 1)
                tt(y_sq_sum[:, j], y_sq_sum[:, j], y_sq[:, j], ALU.add).then_inc(y_att_sq, 1)

            def stage(i, j):
                hc = i * 2 + j
                if due(hc * NT - NT):
                    pool.wait_ge(qk_done, hc * NT - NT)
                for out, part, kind in ((qa[0:DH], 0, 0), (qa[DH:P], 0, 0), (ks[0:DH], 0, 1), (ks[DH:P], 1, 1),
                                        (ql[0:DH], 1, 0)):
                    pool.dma_start(out[:, j, :], qk_heads[part, 2 * j + kind, i]).then_inc(staged[j], 16)

            def values_low(i, j):
                pool.wait_ge(values_high_done, i * 2 + (j + 1))
                tt(vs[:, j, :, DH:P], vv[:, j, :, :], vs[:, j, :, 0:DH].bitcast(f32),
                   ALU.subtract).then_inc(values_low_done, 1)

            for j in range(2):
                pool.wait_ge(qk_out[j], 2 * 16 * 2)
            pool.wait_ge(y_ssm_sq, 1)
            for j in range(2):
                stage(0, j)
                qk_low_parts(10 + j, j)
            values_low(0, 0)
            pool.wait_ge(mm_done, 2 * C_OUT)
            link(pool.memset(y_sq_sum[:], 0.0))
            values_low(0, 1)
            for j in range(2):
                pool.wait_ge(qk_out[j], 2 * 16 * NH)
            stage(1, 0)
            with pool.Fori(1, NH - 1) as i:
                for j in range(2):
                    values_low(i, j)
                    head_squares(i - 1, j)
                    stage(*((i, 1) if j == 0 else (i + 1, 0)))
            values_low(NH - 1, 0)
            head_squares(NH - 2, 0)
            stage(NH - 1, 1)
            values_low(NH - 1, 1)
            head_squares(NH - 2, 1)
            head_squares(NH - 1, 0)

            def add_squares(squares, acc, sq, h, k):
                count = h * (KT - 1) + k
                pool.wait_ge(squares.sq, h * KT + k + 1)
                if count > 1:
                    pool.wait_ge(squares.added, count - 1)
                a = sq[:, 0, half(h)] if k == 1 else acc[:, half(h)]
                tt(acc[:, half(h)], a, sq[:, k % 2, half(h)], ALU.add).then_inc(squares.added, 1)

            def add_residual_squares(h, k):
                n = h * KT + k
                pool.wait_ge(h2_squares.sq, n + 1)
                if n:
                    pool.wait_ge(h2_squares.added, n)
                tt(acc2b[:, half(h)], acc2b[:, half(h)], sq2b[:, n % 2, :], ALU.add).then_inc(h2_squares.added, 1)

            for k in range(1, KT):
                add_squares(zo_squares, acc2, sq2, 0, k)
            link(pool.memset(acc2b[:], 0.0))
            for n in range(KT):
                if n >= 3:
                    add_residual_squares(0, n - 3)
                if n:
                    add_squares(zo_squares, acc2, sq2, 1, n)
            for k in range(KT - 3, KT):
                add_residual_squares(0, k)
            for k in range(KT):
                add_residual_squares(1, k)

            for p_, n in enumerate(PARTS):
                f0 = sum(PARTS[:p_])
                with pool.Fori(0, n) as i:
                    for h in range(2):
                        pool.wait_ge(hid_high, i * 2 + (2 * f0 + h + 1))
                        pool.wait_ge(x2_out, 16 * 2)
                        tt(hid_lo[:, i, half(h)], hf[:, half(h)], hid_hi[:, i, half(h)].bitcast(f32),
                           ALU.subtract).then_inc(hid_low, 1)
            for h in range(2):
                for k in range(1, KT):
                    add_squares(ff_squares, r1["acc3"], r1["sq3"], h, k)
            pool.wait_ge(ne_norm.rstd, 2)
            pool.wait_ge(x2_again, 16 * KT)
            for k in range(OUT_DVE, KT):
                pool.wait_ge(z_gained, k + 1 - OUT_DVE)
                link(tt(z[:, k, half(1)], z[:, k, half(1)], rb[:, half(1)], ALU.mult))
                tt(z[:, k, half(1)], z[:, k, half(1)], r1["x2r"][:, k, half(1)], ALU.add).then_inc(out_done_pool, 1)

        @block.tensor
        def _(pe):
            pe.wait_ge(x_high, 1)
            pe.wait_ge(uf_high, 1)
            for s in range(TS):
                pe.matmul(ps[:, s, 0:UF], op_hi_c[:, 0, s, :], ufh[:, 0, :], start=True, stop=False)
            for k in range(KT):
                pe.wait_ge(x_split, k + 1)
                pe.wait_ge(uf_split, k // 2 + 1)
                for s in range(TS):
                    out = ps[:, s, 0:UF]
                    if k:
                        pe.matmul(out, op_hi_c[:, k, s, :], ufh[:, k, :], start=False, stop=False)
                    pe.matmul(out, op_hi_c[:, k, s, :], ufl[:, k, :], start=False, stop=False)
                    last = pe.matmul(out, op_lo_c[:, k, s, :], ufh[:, k, :], start=False, stop=k == KT - 1)
            last.then_inc(uf_mm, 1)

            def token_sums():
                pe.wait_ge(uf_copied, 1 + TS)
                pe.wait_ge(sq_added, KT - 1)
                pe.wait_ge(ones_set, 1)
                acc1_c = acc1[:].rearrange("p (c t) -> p t c", t=TS)
                for m in range(NT):
                    pe.matmul(ps[:, 2, m:m + 1], acc1[:, m * P:(m + 1) * P], ones[:, 0:1], start=True, stop=True)
                for t in range(TS):
                    last = pe.matmul(ps[:, 2, NT + t:NT + t + 1], acc1_c[:, t, :], ones[:, 0:1], start=True, stop=True)
                last.then_inc(n1s_norm.sums, 1)

            for w in range(NV):
                pe.wait_ge(v_split, w + 1)
                for m in range(NT):
                    if w == 0 and m < 4:
                        pe.wait_ge(uf_copied, 2 + m)
                    if w == 0 and m == 1:
                        token_sums()
                    if w == 0 and m == 4:
                        for h in range(2):
                            norm_sums(pe, n1_norm, acc1, 0, h)
                    if due(NT * w + m - 3):
                        pe.wait_ge(v_scaled, NT * w + m - 3)
                    out = ps[:, 4 + m % 4, 0:VW]
                    tok = slice(m * P, (m + 1) * P)
                    for k in range(KT):
                        pe.matmul(out, op_hi[:, k, tok], vh[:, w % 2, k, :], start=k == 0, stop=False)
                        pe.matmul(out, op_hi[:, k, tok], vl[:, w % 2, k, :], start=False, stop=False)
                        last = pe.matmul(out, op_lo[:, k, tok], vh[:, w % 2, k, :], start=False, stop=k == KT - 1)
                    last.then_inc(v_mm, 1)
            pe.wait_ge(ident_set, 1)
            pe.wait_ge(uf_scaled, 1)
            pe.wait_ge(n1s_norm.mean, 1)
            for s in range(TS):
                last = pe.transpose(ps[0:NH, 2 + s // 4, (s % 4) * P:(s % 4 + 1) * P], fl[:, s, :], ident[:])
            last.then_inc(f_mm, 1)
            pe.wait_ge(v_scaled, NV * NT)
            for a in range(4):
                for b in range(4):
                    g = 4 * a + b
                    last = pe.transpose(ps[:, 4 + a, b * P:(b + 1) * P],
                                        ug[:, g, :, :].rearrange("p t c -> p (t c)"), ident[:])
                last.then_inc(ut_mm, 1)
            pe.wait_ge(n1_norm.mean, 1)
            pe.wait_ge(f_abs, 1)

            def qk_step(c, m, j, n):
                chunk_products(pe, c, j, op_hi, op_lo)

            steps(pe, 0, 4, qk_step, peel=4)
            pe.wait_ge(mt_done, 1)
            pe.wait_ge(ut_out, 1)
            for a in range(4):
                for b in range(4):
                    last = pe.transpose(ps[:, 4 + a, b * P:(b + 1) * P], mt[:, a // 2, 4 * (a % 2) + b, :], ident[:])
                last.then_inc(mb_mm, 1)
            pe.wait_ge(mb_out, 1)
            pe.wait_ge(d_done, 1)
            for a in range(4):
                for b in range(4):
                    g = group_at(a, b)
                    r, j = slice(ST * (g % 2), ST * (g % 2 + 1)), g // 2
                    out = ps[0:CH, 4 + a, b * P:(b + 1) * P]
                    pe.matmul(out, bbar[r, 0, j, :], dre[r, j, 0:TS, :], start=True, stop=False)
                    last = pe.matmul(out, bbar[r, 1, j, :], dim_[r, j, 0:TS, :], start=False, stop=True)
                last.then_inc(kl_mm, 1)
            pe.wait_ge(kl_out, 1)
            for r in range(2):
                for g in range(G):
                    j, rows_ = g // 2, slice(ST * (g % 2), ST * (g % 2 + 1))
                    last = pe.matmul(ps[rows_, 4 + 2 * r + j // 4, (j % 4) * NC:(j % 4 + 1) * NC],
                                     mb[:, r, j, rows_], ut[:, g, :], start=True, stop=True)
            last.then_inc(x_mm, 1)
            steps(pe, 4, 8, qk_step)
            pe.wait_ge(h_done, 1)
            pe.wait_ge(tz_in, 16 * TS)
            for g in range(G):
                j, r = g // 2, slice(ST * (g % 2), ST * (g % 2 + 1))
                a, b = bank_of(g)
                out = ps[:, 4 + a, b * P:(b + 1) * P]
                pe.matmul(out, ut[:, g, :], tz[:, g, :], start=True, stop=False)
                pe.matmul(out, hs[r, 0, j, :], dre[r, j, 1:TS + 1, :], start=False, stop=False)
                last = pe.matmul(out, hs[r, 1, j, :], dim_[r, j, 1:TS + 1, :], start=False, stop=True)
            last.then_inc(y_mm, 1)
            steps(pe, 8, 10, qk_step)
            pe.wait_ge(gelu_done, 1)
            for a in range(4):
                for b in range(4):
                    t, k = (4 * a + b) // 2, (4 * a + b) % 2
                    last = pe.transpose(ps[:, 4 + a, b * P:(b + 1) * P], yn[:, t, k * P:(k + 1) * P], ident[:])
                last.then_inc(gt_mm, 1)
            pe.wait_ge(gt_out, 1)
            pe.wait_ge(wg_in, 16)
            for t in range(TS):
                for k in range(2):
                    last = pe.matmul(ps[:, 4 + t // 2, (t % 2) * SSM_W:(t % 2 + 1) * SSM_W], gt[:, 2 * t + k, :],
                                     wg[:, k, :], start=k == 0, stop=k == 1)
            last.then_inc(glu_mm, 1)

            steps(pe, 10, 12, qk_step)

            pe.wait_ge(glu_sum, 1)
            pe.wait_ge(evacuated, 2 * C_OUT)

            def scores(i, j, g, r):
                u, w = unit(i, j, g), (g + 1) * QB * P
                if g == ORDER[0] and r == 0:
                    pe.wait_ge(staged[j], i * 80 + 80)
                if due(u * 2 + (r - 1)):
                    pe.wait_ge(row_max_done, u * 2 + (r - 1))
                qs = slice((QB * g + r) * P, (QB * g + r + 1) * P)
                for b in range(-(-w // HALF)):
                    n = min(HALF, w - b * HALF)
                    out, key = ps[:, 2 * r + b, 0:n], slice(b * HALF, b * HALF + n)
                    masked = j == 1 and b == (w - 1) // HALF
                    pe.matmul(out, qa[:, j, qs], ks[:, j, key], start=True, stop=False)
                    last = pe.matmul(out, ql[0:DH, j, qs], ks[0:DH, j, key], start=False, stop=not masked)
                    if masked:
                        last = pe.matmul(ps[:, 2 * r + b, n - QB * P:n], ident_b[:], mask_b[:, r, :],
                                         start=False, stop=True)
                last.then_inc(qk_done, 1)

            def transposed(i, j, g, b):
                pc, slot = piece(i, j, g, b), slot_of(j, g, b)
                if b == 0:
                    pe.wait_ge(exp_done, unit(i, j, g) * 2 + 2)
                if due(pc - 1):
                    pe.wait_ge(pt_low_done, pc - 1)
                for a in range(2):
                    for r in range(QB):
                        last = pe.transpose(ps[:, 4 + slot % 2, (a * QB + r) * P:(a * QB + r + 1) * P],
                                            probs(g, r)[:, (2 * b + a) * P:(2 * b + a + 1) * P], ident[:])
                last.then_inc(pt_mm, 1)

            def outputs(i, j, g, b):
                slot = slot_of(j, g, b)
                if b == 0:
                    if due(unit(i, j, g) - 1):
                        pe.wait_ge(y_done, unit(i, j, g) - 1)
                    if g == ORDER[0]:
                        pe.wait_ge(values_low_done, i * 2 + (j + 1))
                pe.wait_ge(pt_low_done, piece(i, j, g, b) + 1)
                for a in range(2):
                    pe.matmul(outputs_bank(g), vs[:, j, 2 * b + a, :], pth[:, slot % 4, a, :],
                              start=b == 0 and a == 0, stop=False)
                    last = pe.matmul(outputs_bank(g), vs[:, j, 2 * b + a, :], ptl[:, slot % 4, a, :], start=False,
                                     stop=b == g and a == 1)
                last.then_inc(pv_done, 1)

            def y_back(i, j, g):
                pe.wait_ge(ot_done, unit(i, j, g) + 1)
                for r in range(QB):
                    last = pe.matmul(y_bank(g, r), ot[:, PLACE[g] % 2, r * P:(r + 1) * P], ident2[:], start=True, stop=True)
                last.then_inc(yt_mm, 1)

            def pe_unit(i, j, g, ahead_, prev, on, last):
                for b in range(max(g + 1, QB)):
                    if b < QB and ahead_:
                        scores(*ahead_, b)
                    if b <= g and on[b]:
                        transposed(*on[b])
                    if b <= g:
                        outputs(i, j, g, b)
                    if b == min(g, 1) and prev:
                        y_back(*prev)

            for g in ORDER[:2]:
                for r in range(QB):
                    scores(0, 0, g, r)
            for n in range(2):
                transposed(0, *PIECES[n])
            bodies(pe, pe_unit)
            y_back(NH - 1, *BODY[-1])

            def mix_transposed(n):
                k, h = MIX[n]
                if due(n - 3):
                    pe.wait_ge(mix_split, n - 3)
                for a in range(4):
                    m = 4 * h + a
                    if k < SSM_W // P:
                        src = yn[:, m, k * P:(k + 1) * P]
                    else:
                        src = ya_flat[:, m, (k - 2) * P:(k - 1) * P]
                    last = pe.transpose(ps[:, 4 + n % 4, a * P:(a + 1) * P], src, ident[:])
                last.then_inc(mix_mm, 1)

            pe.wait_ge(y_scaled, 1)
            pe.wait_ge(y_done, 2 * NH * UNITS)
            for n in range(4):
                mix_transposed(n)
            pe.wait_ge(y_scaled, 2)
            pe.wait_ge(fox_scaled, 1)
            for n in range(4, MIX_FIRST):
                mix_transposed(n)
            pe.wait_ge(mix_split, MIX_FIRST)

            def rest_of_mix(k):
                if k == 1:
                    pe.wait_ge(y_scaled, 3)
                    pe.wait_ge(fox_scaled, 2)
                if k in range(1, 1 + len(MIX) - MIX_FIRST):
                    mix_transposed(MIX_FIRST + k - 1)

            half_products(pe, C_OUT, 0, 0, op_hi, op_lo, before=rest_of_mix)
            half_products(pe, C_OUT + 1, 1, 0, op_hi, op_lo)
            steps(pe, C_OUT + 2, C_OUT2, lambda c, m, j, n: half_products(pe, c, j, 0, op_hi, op_lo))
            pe.wait_ge(mix_split, len(MIX))

            def first_half_sums(k):
                if k == 6:
                    pe.wait_ge(zo_squares.added, KT - 1)
                    norm_sums(pe, no_norm, acc2, 4, 0)

            half_products(pe, C_OUT2, 0, 1, op_hi, op_lo, before=first_half_sums)
            half_products(pe, C_OUT2 + 1, 1, 1, op_hi, op_lo)
            steps(pe, C_OUT2 + 2, C_FFN, lambda c, m, j, n: half_products(pe, c, j, 1, op_hi, op_lo))

            def first_tile(j, h, before):
                c = C_FFN + j
                pe.wait_ge(w_split, c + 1)
                pe.wait_ge(evacuated, 2 * (c - 1))
                for k in range(KT):
                    before(k)
                    out = ps[:, 2 * j + h, :]
                    pe.matmul(out, w_hi[:, j, k, :], op_hi[:, k, half(h)], start=k == 0, stop=False)
                    pe.matmul(out, w_hi[:, j, k, :], op_lo[:, k, half(h)], start=False, stop=False)
                    last = pe.matmul(out, w_lo[:, j, k, :], op_hi[:, k, half(h)], start=False, stop=k == KT - 1)
                last.then_inc(mm_done, 1)

            def first_half_ready(k):
                pe.wait_ge(h2_split, k + 1)
                if k == 4:
                    pe.wait_ge(zo_squares.added, 2 * (KT - 1))
                    norm_sums(pe, no_norm, acc2, 4, 1)
                if k == 6:
                    pe.wait_ge(h2_squares.added, KT)
                    pe.matmul(ps[:, 6, :], ones[:], acc2b[:, half(0)], start=True, stop=True).then_inc(nf_norm.sums, 1)

            def last_half_sums(k):
                if k == 4:
                    pe.wait_ge(h2_squares.added, 2 * KT)
                    pe.matmul(ps[:, 7, :], ones[:], acc2b[:, half(1)], start=True, stop=True).then_inc(nf_norm.sums, 1)

            first_tile(0, 0, first_half_ready)
            first_tile(1, 0, lambda k: None)
            first_tile(0, 1, lambda k: pe.wait_ge(h2_split, KT + k + 1))
            first_tile(1, 1, last_half_sums)
            chunk_products(pe, C_FFN + 2, 0, op_hi, op_lo, late=1)
            chunk_products(pe, C_FFN + 3, 1, op_hi, op_lo)
            for p_, n in enumerate(PARTS[:-1]):
                gu, dn = BASES[p_]
                steps(pe, gu + (4 if p_ == 0 else 0), dn, qk_step)
                done = 2 * sum(PARTS[:p_ + 1])

                def down(c, m, j, n_, done=done, nk=PARTS[p_]):
                    def before(h, k):
                        if k == 0:
                            pe.wait_ge(hid_low, done - 2)
                        if k == nk - 1:
                            pe.wait_ge(hid_low, done - 1 + h)
                    chunk_products(pe, c, j, hid_hi, hid_lo, nk=nk, before=before)

                steps(pe, dn, dn + KT, down)
            gu, dn = BASES[-1]
            steps(pe, gu, dn, qk_step)

            def last_tile_ready(k):
                if k == 0:
                    pe.wait_ge(hid_low, 2 * FT - 2)
                if k == PARTS[-1] - 1:
                    pe.wait_ge(hid_low, 2 * FT)

            def last_down(h):
                return lambda c, m, j, n: half_products(pe, c, j, h, hid_hi, hid_lo, nk=PARTS[-1], before=last_tile_ready)

            steps(pe, dn, dn + KT, last_down(0))
            half_products(pe, dn + KT, 0, 1, hid_hi, hid_lo, nk=PARTS[-1])
            pe.wait_ge(ff_squares.added, KT - 1)
            norm_sums(pe, ne_norm, r1["acc3"], 4, 0)
            half_products(pe, dn + KT + 1, 1, 1, hid_hi, hid_lo, nk=PARTS[-1])
            steps(pe, dn + KT + 2, C_END, last_down(1))
            pe.wait_ge(ff_squares.added, 2 * (KT - 1))
            norm_sums(pe, ne_norm, r1["acc3"], 4, 1)
    return nc


def tiles(a):
    return np.ascontiguousarray(a.reshape(-1, P, a.shape[1]).transpose(1, 0, 2))


def chunks(a, width):
    r, c = a.shape
    return a.reshape(r // P, P, c // width, width).transpose(2, 1, 0, 3)


def layout(x, g_pre_mix, w_in, b_f, ssm_log_dt, ssm_a_re, ssm_a_im, ssm_b_re, ssm_b_im, ssm_c_re, ssm_c_im,
           ssm_d, w_glu, b_glu, g_mix, w_out, g_post_mix, g_pre_ffn, w_gate_up, w_down, g_post_ffn):
    w = w_in[0]
    o = SSM_W
    cols = {}
    for kind in ("dsa", "fox"):
        for part in "qkv":
            cols[kind + part] = w[:, o:o + ATT_W]
            o += ATT_W
    forget = w[:, o:o + NH]
    qk = [chunks(cols[n], P) for n in ("dsaq", "dsak", "foxq", "foxk")]
    gate, up = chunks(w_gate_up[0][:, :D_FF], P), chunks(w_gate_up[0][:, D_FF:], P)
    stream = [qk[n][p_] for p_ in range(NH // 2) for n in range(4)] + list(chunks(w_out[0], P))
    f = 0
    for p_, n in enumerate(PARTS):
        for t in range(f, f + n):
            stream += [gate[t], up[t]]
        down = list(chunks(w_down[0][f * P:(f + n) * P], P))
        f += n
        if p_ < len(PARTS) - 1:
            stream += down
    states = lambda a: a[0].reshape(NJ, 2 * ST).T
    by_state = lambda a: a[0].reshape(NJ, 2 * ST, CH).transpose(1, 0, 2)
    log_dt = np.repeat(ssm_log_dt[0][:, None], ST, axis=1)[None]
    lag = np.arange(P)[:, None] - (np.arange(LNC_W)[None, :] - (SEQ - P))
    count = sum(((lag >= 0) & (lag <= w_) & (lag % d == 0)).astype(np.int64) for w_, d in ((128, 1), (512, 4), (2048, 16)))
    lnc = np.where(count > 0, np.log(np.maximum(count, 1)), MASKED).astype(np.float32)
    return {
        "x_t": tiles(x[0].T),
        "gains": np.stack([g[0].reshape(KT, P).T for g in (g_pre_mix, g_mix, g_post_mix, g_pre_ffn, g_post_ffn)], 1),
        "w_uf": tiles(np.concatenate([w[:, :SSM_W], forget], axis=1)),
        "w_v": chunks(np.concatenate([cols["dsav"], cols["foxv"]], axis=1), VW),
        "w_stream": np.stack(stream),
        "w_last": np.stack(down),
        "s_par": np.stack([states(log_dt), states(ssm_a_re), states(ssm_a_im)], 1),
        "s_bc": np.stack([by_state(ssm_b_re), by_state(ssm_b_im), by_state(ssm_c_re.transpose(0, 1, 3, 2)),
                          by_state(ssm_c_im.transpose(0, 1, 3, 2))], 1),
        "rows": np.stack([ssm_d[0], b_glu[0]]),
        "w_glu": tiles(w_glu[0]),
        "b_f": b_f[0][:, None],
        "lnc_dram": lnc,
    }


def kernel(**inputs):
    import concourse.bacc as bacc
    from concourse.bass_utils import run_bass_kernel_spmd

    nc = bacc.Bacc("TRN2", target_bir_lowering=False, num_devices=1)
    arrays = {n: np.ascontiguousarray(a) for n, a in layout(**{n: np.asarray(a) for n, a in inputs.items()}).items()}
    args = {n: nc.dram_tensor(n, a.shape, mybir.dt.from_np(a.dtype), kind="ExternalInput").ap()
            for n, a in arrays.items()}
    out = nc.dram_tensor("out_t", (P, KT, SEQ), mybir.dt.float32, kind="ExternalOutput").ap()
    block_kernel(nc, out_t=out, **args)
    got = run_bass_kernel_spmd(nc, [arrays], core_ids=[0]).results[0]["out_t"]
    return np.ascontiguousarray(got.transpose(1, 0, 2).reshape(D, SEQ).T)[None]
```
